# Optimizing a Trainium2 kernel written in Bass

```python
import jax, jax.numpy as jnp
from jax import lax
import numpy as np

D_MODEL = 2048
BATCH = 1
SEQ = 256
DEPTH = 1
DEC_BATCH = 8
DEC_SEQ = 8
PAST_LEN = 2048
PAGE_SIZE = 128

MIX_WIDTH = D_MODEL
POOL_WIDTH = MIX_WIDTH // 2
POOL_WINDOWS = (2, 4, 8, 16)
POOL_GROUPS = len(POOL_WINDOWS)
POOL_GROUP_DIM = POOL_WIDTH // POOL_GROUPS
POOL_CACHE = max(POOL_WINDOWS) - 1
HG_WIDTH = MIX_WIDTH - POOL_WIDTH
HG_HEAD_DIM = 128
HG_HEADS = HG_WIDTH // HG_HEAD_DIM
CHUNK = 16
D_FF = ((8 * D_MODEL // 3 + 255) // 256) * 256
IN_COLS = POOL_WIDTH + 4 * HG_WIDTH
EPS = 1e-6

kernel_name = "hybrid_pool_hgrn2_decode_step"

def rms_norm(x, g):
    x32 = x.astype(jnp.float32)
    y = x32 * lax.rsqrt(jnp.mean(x32 * x32, axis=-1, keepdims=True) + EPS)
    return (y * g.astype(jnp.float32)).astype(x.dtype)

def pool_mix(u, prev, pos0, w_pool, pool_scale):
    B, T, _ = u.shape
    full = jnp.concatenate([prev.astype(u.dtype), u], axis=1)
    cs = jnp.cumsum(full.astype(jnp.float32), axis=1)
    cs = jnp.concatenate([jnp.zeros((B, 1, POOL_WIDTH), jnp.float32), cs], axis=1)
    end = cs[:, POOL_CACHE + 1:]
    pos = pos0 + jnp.arange(T)
    means = []
    for gi, w in enumerate(POOL_WINDOWS):
        sl = slice(gi * POOL_GROUP_DIM, (gi + 1) * POOL_GROUP_DIM)
        start = cs[:, POOL_CACHE + 1 - w:POOL_CACHE + 1 - w + T, sl]
        cnt = jnp.minimum(pos + 1, w).astype(jnp.float32)[None, :, None]
        means.append((end[..., sl] - start) / cnt)
    pooled = jnp.concatenate(means, axis=-1) - u.astype(jnp.float32)
    pooled = pooled.reshape(B, T, POOL_GROUPS, POOL_GROUP_DIM)
    out = jnp.einsum('btgc,gcd->btgd', pooled, w_pool.astype(jnp.float32))
    out = out.reshape(B, T, POOL_WIDTH) * pool_scale.astype(jnp.float32)
    return out.astype(u.dtype), full[:, -POOL_CACHE:]

def hgrn2_recurrence(q, k, v, logf, S0):
    B, T, H, K = q.shape
    V = v.shape[-1]
    pad = (-T) % CHUNK
    n = (T + pad) // CHUNK

    def prep(a):
        a = jnp.pad(a.astype(jnp.float32), ((0, 0), (0, pad), (0, 0), (0, 0)))
        return a.reshape(B, n, CHUNK, H, a.shape[-1]).transpose(1, 0, 3, 2, 4)

    qs, ks, vs, gs = prep(q), prep(k), prep(v), prep(logf)
    causal = jnp.tril(jnp.ones((CHUNK, CHUNK), bool))[:, :, None]

    def step(S, inp):
        qc, kc, vc, gc = inp
        b = jnp.cumsum(gc, axis=2)
        diff = b[:, :, :, None, :] - b[:, :, None, :, :]
        decay = jnp.exp(jnp.where(causal, diff, -jnp.inf))
        scores = jnp.einsum('bhtk,bhsk,bhtsk->bhts', qc, kc, decay)
        o = (jnp.einsum('bhts,bhsv->bhtv', scores, vc)
             + jnp.einsum('bhtk,bhkv->bhtv', qc * jnp.exp(b), S))
        b_last = b[:, :, -1:, :]
        S = (jnp.exp(b_last[:, :, 0, :])[..., None] * S
             + jnp.einsum('bhsk,bhsv->bhkv', kc * jnp.exp(b_last - b), vc))
        return S, o

    S, o = lax.scan(step, S0.astype(jnp.float32), (qs, ks, vs, gs))
    o = o.transpose(1, 0, 3, 2, 4).reshape(B, n * CHUNK, H, V)[:, :T]
    return o, S

def run_group(x, pool_prev, S_prev, pos0, lbs, norm1, w_in, w_pool, pool_scale,
              hg_norm, w_o, norm2, w_gate, w_up, w_down, norm_f):
    B, T, _ = x.shape
    pools, states = [], []
    for l in range(DEPTH):
        h = rms_norm(x, norm1[l])
        z = h @ w_in[l]
        u, q, f, i, g = jnp.split(
            z, [POOL_WIDTH, POOL_WIDTH + HG_WIDTH, POOL_WIDTH + 2 * HG_WIDTH,
                POOL_WIDTH + 3 * HG_WIDTH], axis=-1)
        pool_out, pool_new = pool_mix(u, pool_prev[l], pos0, w_pool[l], pool_scale[l])
        lb = lbs[l]
        forget = lb + (1.0 - lb) * jax.nn.sigmoid(f.astype(jnp.float32))
        logf = jnp.log(forget)
        k_in = 1.0 - forget
        q_f = jax.nn.silu(q.astype(jnp.float32))
        heads = lambda a: a.reshape(B, T, HG_HEADS, HG_HEAD_DIM)
        o, S_new = hgrn2_recurrence(heads(q_f), heads(k_in), heads(i), heads(logf), S_prev[l])
        o = o * lax.rsqrt(jnp.mean(o * o, axis=-1, keepdims=True) + EPS)
        o = o * hg_norm[l].astype(jnp.float32).reshape(HG_HEADS, HG_HEAD_DIM)
        o = o.reshape(B, T, HG_WIDTH) * jax.nn.silu(g.astype(jnp.float32))
        mix = jnp.concatenate([pool_out, o.astype(x.dtype)], axis=-1) @ w_o[l]
        x = x + mix
        h2 = rms_norm(x, norm2[l])
        x = x + (jax.nn.silu(h2 @ w_gate[l]) * (h2 @ w_up[l])) @ w_down[l]
        pools.append(pool_new)
        states.append(S_new.astype(S_prev.dtype))
    return rms_norm(x, norm_f), jnp.stack(pools), jnp.stack(states)

def setup_inputs(seed: int = 0) -> dict:
    key = jax.random.key(seed)
    ks = jax.random.split(key, 20)
    nrm = lambda k, s, sc: jax.random.normal(k, s, jnp.float32) * sc
    return {
        "x_prompt": nrm(ks[0], (BATCH, SEQ, D_MODEL), 1.0),
        "x_sample": nrm(ks[1], (DEC_BATCH, DEC_SEQ, D_MODEL), 1.0),
        "cache_pool": nrm(ks[2], (DEPTH, DEC_BATCH, POOL_CACHE, POOL_WIDTH), 1.0),
        "state_hgrn": nrm(ks[3], (DEPTH, DEC_BATCH, HG_HEADS, HG_HEAD_DIM, HG_HEAD_DIM), 0.3),
        "lb_param": nrm(ks[4], (DEPTH + 1, HG_WIDTH), 0.1),
        "norm1": 1.0 + nrm(ks[5], (DEPTH, D_MODEL), 0.02),
        "w_in": nrm(ks[6], (DEPTH, D_MODEL, IN_COLS), D_MODEL ** -0.5),
        "w_pool": nrm(ks[7], (DEPTH, POOL_GROUPS, POOL_GROUP_DIM, POOL_GROUP_DIM), POOL_GROUP_DIM ** -0.5),
        "pool_scale": 1.0 + nrm(ks[8], (DEPTH, POOL_WIDTH), 0.02),
        "hg_norm": 1.0 + nrm(ks[9], (DEPTH, HG_WIDTH), 0.02),
        "w_o": nrm(ks[10], (DEPTH, MIX_WIDTH, D_MODEL), MIX_WIDTH ** -0.5),
        "norm2": 1.0 + nrm(ks[11], (DEPTH, D_MODEL), 0.02),
        "w_gate": nrm(ks[12], (DEPTH, D_MODEL, D_FF), D_MODEL ** -0.5),
        "w_up": nrm(ks[13], (DEPTH, D_MODEL, D_FF), D_MODEL ** -0.5),
        "w_down": nrm(ks[14], (DEPTH, D_FF, D_MODEL), D_FF ** -0.5),
        "norm_f": 1.0 + nrm(ks[15], (D_MODEL,), 0.02),
    }

def reference(x_prompt, x_sample, cache_pool, state_hgrn, lb_param, norm1, w_in, w_pool,
              pool_scale, hg_norm, w_o, norm2, w_gate, w_up, w_down, norm_f):
    lbs = jnp.cumsum(jax.nn.softmax(lb_param.astype(jnp.float32), axis=0), axis=0)
    weights = (norm1, w_in, w_pool, pool_scale, hg_norm, w_o, norm2, w_gate, w_up, w_down, norm_f)
    pool_zero = jnp.zeros((DEPTH, BATCH, POOL_CACHE, POOL_WIDTH), x_prompt.dtype)
    state_zero = jnp.zeros((DEPTH, BATCH, HG_HEADS, HG_HEAD_DIM, HG_HEAD_DIM), state_hgrn.dtype)
    y_prompt, pool_state_prompt, hgrn_state_prompt = run_group(
        x_prompt, pool_zero, state_zero, 0, lbs, *weights)
    y_sample, pool_state_sample, hgrn_state_sample = run_group(
        x_sample, cache_pool, state_hgrn, PAST_LEN, lbs, *weights)
    return (y_prompt, y_sample, pool_state_prompt, hgrn_state_prompt, pool_state_sample, hgrn_state_sample)


_drawn_inputs = setup_inputs


def setup_inputs(seed=0):
    import zlib

    import numpy as np

    out = dict(_drawn_inputs(seed))
    spreads = {}
    factors = {'pool_scale': 5.481, 'hg_norm': 7.692, 'norm2': 4.665, 'norm_f': 2.739}
    for name, (base, spread) in spreads.items():
        noise = np.random.default_rng([zlib.crc32(name.encode()), seed]).standard_normal(out[name].shape)
        drawn = base * np.exp(spread * noise) if base else spread * noise
        out[name] = __import__('jax').numpy.asarray(drawn.astype(out[name].dtype))
    for name, factor in factors.items():
        out[name] = (out[name] * factor).astype(out[name].dtype)
    return out
```

```python
from contextlib import ExitStack

import concourse.bass as bass
from concourse import mybir

F32 = mybir.dt.float32
F32R = mybir.dt.float32r
BF16 = mybir.dt.bfloat16
U32 = mybir.dt.uint32
ALU = mybir.AluOpType
ACT = mybir.ActivationFunctionType
MUL, ADD, SUB = ALU.mult, ALU.add, ALU.subtract

P = 128
D = 2048
KD = D // P
TP, NB, TS = 256, 8, 8
NS = NB * TS
N = TP + NS
CH = 128
NC = TP // CH
PW = 1024
WINDOWS = (2, 4, 8, 16)
NG = len(WINDOWS)
GC = PW // NG
CACHE = max(WINDOWS) - 1
HEADS = 8
FF = 5632
KF = FF // P
BLOCKS = 4
KB = KF // BLOCKS
EPS = 1e-6
LP, LS = 7, 3

PARAMS = (("norm1", KD), ("norm2", KD), ("norm_f", KD), ("lb_param", 2 * HEADS),
          ("pool_scale", PW // P), ("hg_norm", HEADS))
C_ID = 0
C_MP = C_ID + P
C_MS = C_MP + LP * P
C_BM = C_MS + LS * (NS // 2)
C_IC = C_BM + NB
C_END = C_IC + NG * 16

U0 = 0
H0 = PW // P
G0 = H0 + 3 * HEADS
O0 = G0 + HEADS
F0 = O0 + KD
PER_BLOCK = 2 * KB + KD

PUTS = LP + LS + 2


def constant_table(np):
    c = np.zeros((P, C_END), np.float32)
    c[:, C_ID:C_ID + P] = np.eye(P)
    s = np.arange(P)[:, None]
    for level in range(LP):
        half, size = 2 ** level, 2 ** (level + 1)
        t = np.array([t for t in range(CH) if t % size >= half])[None, :]
        m = ((s // size == t // size) & (s % size < half)).astype(np.float32)
        for ch in range(NC):
            c[:, C_MP + level * P + ch * 64:C_MP + level * P + ch * 64 + 64] = m
        if level < LS:
            c[:NS, C_MS + level * 32:C_MS + level * 32 + 32] = m[:NS, :32]
    for b in range(NB):
        c[b * TS:(b + 1) * TS, C_BM + b] = 1
    for g, w in enumerate(WINDOWS):
        c[:, C_IC + 16 * g:C_IC + 16 * g + 16] = 1 / np.minimum(np.arange(16) + 1, w).astype(np.float32)
    return c


def hybrid_kernel(nc, x_prompt, x_sample, cache_pool, state_hgrn, lb_param, norm1, w_in, w_pool, pool_scale,
                  hg_norm, w_o, norm2, w_gate, w_up, w_down, norm_f, consts,
                  y_prompt, y_sample, pool_prompt, hgrn_prompt, pool_sample, hgrn_sample):
    param_of = {"norm1": norm1, "norm2": norm2, "norm_f": norm_f, "lb_param": lb_param,
                "pool_scale": pool_scale, "hg_norm": hg_norm}

    def by_rows(w):
        return w.rearrange("(k p) c -> p k c", p=P)

    win_v, wo_v = by_rows(w_in[0]), by_rows(w_o[0])
    wg_v, wu_v, wd_v = by_rows(w_gate[0]), by_rows(w_up[0]), by_rows(w_down[0])

    ctx = ExitStack()
    with ctx:
        def keep(name, shape, dt=F32):
            return ctx.enter_context(nc.sbuf_tensor(name, shape, dt))

        def region(stack, tensors):
            return [stack.enter_context(nc.sbuf_tensor(n, s, d)) for n, s, d in tensors]

        def passing(tensors):
            with ExitStack() as st:
                return region(st, tensors)

        def sem(name):
            return ctx.enter_context(nc.semaphore(name))

        x1 = keep("x_res", [P, KD, N])
        a_hi = keep("a_hi", [P, KD, N], F32R)
        a_lo = keep("a_lo", [P, KD, N], F32R)
        raw = keep("w_raw", [P, 2, KD * P])
        whi = keep("w_hi", [P, 2, KD * P], F32R)
        wlo = keep("w_lo", [P, 2, KD * P], F32R)
        cst = keep("cst", [P, C_END])
        n_par = sum(r for _, r in PARAMS)
        par = keep("par", [P, n_par])
        prow = keep("prow", [n_par, P])
        ones = keep("ones_mat", [P, P])
        meanc = keep("mean_cols", [P, 2])
        rbc = keep("rms_bc", [P, N])
        stat = keep("stat", [P, 12])
        lbt = keep("lb_tmp", [P, 6, HEADS])
        epst = keep("eps_col", [P, 1])

        h_hi, h_lo = passing([("h_hi", [P, KB, N], F32R), ("h_lo", [P, KB, N], F32R)])
        bp_hi = keep("mp_hi", [P, HEADS, N], F32R)
        bp_lo = keep("mp_lo", [P, HEADS, N], F32R)
        wp, cache_t, st_s, st_p = passing([
            ("wp", [P, NG, 2, GC], F32), ("cache_t", [NB * CACHE, PW], F32),
            ("st_s", [NB * CACHE, PW], F32), ("st_p", [CACHE, PW], F32)])
        bh_hi = keep("mh_hi", [P, HEADS, N], F32R)
        bh_lo = keep("mh_lo", [P, HEADS, N], F32R)

        xt, = passing([("xt", [P, 3, D], F32)])
        zg, sg, zu, hid, sq, acc, x2, x2g = passing([
            (n, [P, N], F32) for n in ("zg", "sg", "zu", "hid", "sq", "acc")] + [
            ("x2", [P, 2, N], F32), ("x2g", [P, 2, N], F32)])
        with ExitStack() as st:
            region(st, [("pad_ffn", [P, 10 * N], F32)])
            yt, = region(st, [("yt", [P, 3, D], F32)])
        early = ExitStack()
        zf, = region(early, [("zf", [P, N], F32)])
        zq, sgm, qq = region(early, [(n, [P, N], F32) for n in ("zq", "sgm", "qq")])
        tl = region(early, [(f"t{l}", [P, (N if l <= LS else TP) // 2 ** (l + 1), 4], F32) for l in range(LP + 1)])
        qr = region(early, [(f"qr{l}", [P, N if l <= LS else TP], F32) for l in range(LP + 1)])
        kx = region(early, [(f"kx{l}", [P, N if l <= LS else TP], F32) for l in range(LP + 1)])
        junk, = passing([("junk", [P, 1024], BF16)])
        UW = CACHE + TP + NB * (CACHE + TS)
        uu, wa, wb, pooled, tails = passing([
            ("uu", [P, 2, 2, UW], F32), ("wa", [P, 2, UW], F32), ("wb", [P, 2, UW], F32), ("pooled", [P, 2, N], F32),
            ("tails", [P, 2, NB * CACHE + CACHE], F32)])
        late = ExitStack()
        vv, osq, osb, on = region(late, [(n, [P, N], F32) for n in ("vv", "osq", "osb", "on")])
        vt, kt = region(late, [("vt", [P, 3, P], F32), ("kt", [P, 3, P], F32)])
        sc, scs = region(late, [("sc", [P, NC, CH], F32), ("scs", [NS, NS], F32)])
        s0, sn = region(late, [("s0", [P, NB, P], F32), ("sn", [P, NB, P], F32)])
        vm, = region(late, [("vm", [NS, NB, P], F32)])
        s1, s2, dg = region(late, [("s1", [P, P], F32), ("s2", [P, P], F32), ("dg", [P, N], F32)])
        go = vv
        late.close()
        early.close()

        bank = [ctx.enter_context(nc.psum_tensor(f"bank{i}", [P, 512], F32)) for i in range(8)]
        zb, (SA, SB, SC, TV, TK, OT) = bank[:2], bank[2:]

        ident = cst[:, C_ID:C_ID + P]

        def pcol(name, i):
            at = 0
            for n, r in PARAMS:
                if n == name:
                    return par[:, bass.ds(i + at, 1)]
                at += r

        raw_loaded = [sem("raw_loaded0"), sem("raw_loaded1")]
        hi_ready, lo_ready, piece_used, unit_read = (sem(n) for n in ("hi_ready", "lo_ready", "piece_used", "unit_read"))
        cst_loaded, par_loaded, wp_loaded, cache_loaded, s0_loaded = (
            sem(n) for n in ("cst_loaded", "par_loaded", "wp_loaded", "cache_loaded", "s0_loaded"))
        x_loaded = [sem(f"x_loaded{i}") for i in range(3)]
        fill_done, par_t, par_ready, lb_max, lb_exp, lb_ready = (
            sem(n) for n in ("fill_done", "par_t", "par_ready", "lb_max", "lb_exp", "lb_ready"))
        dve_link, newton_step = sem("dve_link"), sem("newton_step")
        ss_ready, rms_std, rms_diag, rms_bcast, rms_ready, stat_mm = (
            sem(n) for n in ("ss_ready", "rms_std", "rms_diag", "rms_bcast", "rms_ready", "stat_mm"))
        xt_t, xres_act, xres_dve, ahi_ready, alo_ready = (
            sem(n) for n in ("xt_t", "xres_act", "xres_dve", "ahi_ready", "alo_ready"))
        t_ones, tails_ready, sc_zero, acc_zero, pad_zero, cache_tr, cache_in, win_step, win_ready, fix_ready, pooled_ready = (
            sem(n) for n in ("t_ones", "tails_ready", "sc_zero", "acc_zero", "pad_zero", "cache_tr", "cache_in", "win_step", "win_ready", "fix_ready",
                             "pooled_ready"))
        pool_mm, mp_hi_s, mp_lo_s, st_tr, st_copied, out_done = (
            sem(n) for n in ("pool_mm", "mp_hi_s", "mp_lo_s", "st_tr", "st_copied", "out_done"))
        zf_sig, f_ready, prod_ready, zq_sig, q_ready, qr_ready, kx_ready = (
            sem(n) for n in ("zf_sig", "f_ready", "prod_ready", "zq_sig", "q_ready",
                             "qr_ready", "kx_ready"))
        v_tr, k_tr, vt_ready, kt_ready, vm_ready, sc_mm, sc_put, put_go = (
            sem(n) for n in ("v_tr", "k_tr", "vt_ready", "kt_ready", "vm_ready", "sc_mm", "sc_put", "put_go"))
        st_mm, s1_ready, s2_ready, s2_stored, sdec_ready, sn_mm, sn_ready, sn_stored = (
            sem(n) for n in ("st_mm", "s1_ready", "s2_ready", "s2_stored", "sdec_ready", "sn_mm", "sn_ready", "sn_stored"))
        o_mm, o_read, ostat_mm, ostd, orec, odiag, obc_mm, on_ready, mh_hi_s, mh_lo_s = (
            sem(n) for n in ("o_mm", "o_read", "ostat_mm", "ostd", "orec", "odiag", "obc_mm", "on_ready", "mh_hi_s",
                             "mh_lo_s"))
        g_sig, g_act, osum, gated, gm_hi, gm_lo = (
            sem(n) for n in ("g_sig", "g_act", "osum", "gated", "gm_hi", "gm_lo"))
        x1_sq, x1_acc, h2_hi, h2_lo = (sem(n) for n in ("x1_sq", "x1_acc", "h2_hi", "h2_lo"))
        gate_act, hid_ready, hid_hi, hid_lo = (
            sem(n) for n in ("gate_act", "hid_ready", "hid_hi", "hid_lo"))
        x2_scaled, x2_sq, x2_acc, y_tr, y_copied, y_rec, y_scaled_a, y_scaled_v = (
            sem(n) for n in ("x2_scaled", "x2_sq", "x2_acc", "y_tr", "y_copied", "y_rec", "y_scaled_a",
                             "y_scaled_v"))

        block = ctx.enter_context(nc.Block())

        def after(eng, semaphore, value):
            if not isinstance(value, int) or value > 0:
                eng.wait_ge(semaphore, value)

        HALF = ((0, 8), (8, 16))
        HALF_D = ((0, 8), (8, KB))

        def blocks_of(ap, level, n):
            return ap[:, 0:n].rearrange("p (m a j) -> p m a j", a=2, j=2 ** level)

        def times(level, n, lo):
            m = n // 2 ** (level + 1)
            return tl[level][:, 0:m, lo:lo + 2].unsqueeze(3).to_broadcast([P, m, 2, 2 ** level])

        def prod_in(level, which):
            m = (N if level < LS else TP) // 2 ** (level + 1)
            return tl[level][:, 0:m, which:which + 1].rearrange("p (m a) q -> p m (a q)", a=2)

        def right_half(ap, level):
            return ap.rearrange("p (m a j) -> p m a j", a=2, j=2 ** level)[:, :, 1, :]

        def load_params(eng, some):
            at = 0
            for name, rows in PARAMS:
                if (name, rows) in some:
                    src = param_of[name]
                    src = src.rearrange("(r p) -> r p", p=P) if name == "norm_f" else src.rearrange("l (r p) -> (l r) p", p=P)
                    eng.dma_start(prow[at:at + rows, :], src).then_inc(par_loaded, 16)
                at += rows

        @block.sync
        def _(sp):
            def load(n, par_, view, tiles, col):
                after(sp, lo_ready, 2 * n - 2)
                k0, nk = tiles
                sp.dma_start(raw[:, par_, 0:nk * P].rearrange("p (k c) -> p k c", c=P),
                             view[:, bass.ds(k0, nk), bass.ds(col, P)]).then_inc(raw_loaded[par_], 16)

            load_params(sp, PARAMS[:3])
            sp.dma_start(cst[:, :], consts[:, :]).then_inc(cst_loaded, 16)
            sp.dma_start(xt[:, 0, :], x_prompt[0, 0:P, :]).then_inc(x_loaded[0], 16)
            load(0, 0, win_v, (0, KD), 0)
            load(1, 1, win_v, (0, KD), P)
            sp.dma_start(cache_t[:, :], cache_pool[0].rearrange("b t c -> (b t) c")).then_inc(cache_loaded, 16)
            sp.dma_start(wp[:, :, :, :], w_pool[0].rearrange("g (k p) d -> p g k d", p=P)).then_inc(wp_loaded, 16)
            with sp.Fori(1, (H0 // 2)) as i:
                for k in range(2):
                    load(2 * i + k, k, win_v, (0, KD), (2 * i + k) * P)
            with sp.Fori(0, HEADS // 2) as i:
                for k in range(2):
                    for j, part in enumerate((2, 1, 3)):
                        load(H0 + 6 * i + 3 * k + j, (3 * k + j) % 2, win_v, (0, KD),
                             part * PW + (2 * i + k) * P)
            with sp.Fori(0, HEADS // 2) as i:
                for k in range(2):
                    load(G0 + 2 * i + k, k, win_v, (0, KD), 4 * PW + (2 * i + k) * P)
            with sp.Fori(0, KD // 2) as i:
                for k in range(2):
                    load(O0 + 2 * i + k, k, wo_v, (0, KD), (2 * i + k) * P)
            with sp.Fori(0, BLOCKS) as b:
                with sp.Fori(0, KB) as j:
                    for k, view in enumerate((wg_v, wu_v)):
                        load(F0 + PER_BLOCK * b + 2 * j + k, k, view, (0, KD), (b * KB + j) * P)
                with sp.Fori(0, KD // 2) as j:
                    for k in range(2):
                        load(F0 + 2 * KB + PER_BLOCK * b + 2 * j + k, k, wd_v, (b * KB, KB), (2 * j + k) * P)
            sp.wait_ge(s2_stored, 16 * HEADS)
            sp.wait_ge(sn_stored, 16 * HEADS)
            sp.wait_ge(out_done, 16 * (2 + 5))

        @block.tensor
        def _(pe):
            def unit(n, par_, rhs, halves=HALF, between=(None, None), tile_wait=None):
                after(pe, unit_read, n - 1)
                last_k = halves[1][1] - 1
                for p, (k0, k1) in enumerate(halves):
                    pe.wait_ge(hi_ready, 2 * n + p + 1)
                    pe.wait_ge(lo_ready, 2 * n + p + 1)
                    for k in range(k0, k1):
                        if tile_wait is not None:
                            tile_wait(k)
                        r_hi, r_lo = rhs(k)
                        cols = slice(k * P, (k + 1) * P)
                        out = zb[par_][:, 0:N]
                        pe.matmul(out, whi[:, par_, cols], r_hi, start=(k == 0), stop=False)
                        pe.matmul(out, whi[:, par_, cols], r_lo, start=False, stop=False)
                        last = pe.matmul(out, wlo[:, par_, cols], r_hi, start=False, stop=(k == last_k))
                    last.then_inc(piece_used, 1)
                    if between[p] is not None:
                        between[p]()

            def a_rhs(k):
                return a_hi[:, k, :], a_lo[:, k, :]

            def m_rhs(k):
                if k < HEADS:
                    return bp_hi[:, k, :], bp_lo[:, k, :]
                return bh_hi[:, k - HEADS, :], bh_lo[:, k - HEADS, :]

            def h_rhs(k):
                return h_hi[:, k, :], h_lo[:, k, :]

            def token_stats(out_bank, src, which, signal):
                for i, (t0, t1) in enumerate(((0, P), (P, TP), (TP, N))):
                    last = pe.matmul(out_bank[0:t1 - t0, i:i + 1], src[:, t0:t1], meanc[:, which:which + 1],
                                     start=True, stop=True)
                last.then_inc(signal, 1)

            def to_all(out_bank, signal):
                pe.matmul(out_bank[:, 0:TP].rearrange("p (c t) -> p c t", c=2)[:, 0, :], ones[:, :], dg[:, 0:P],
                          start=True, stop=True)
                pe.matmul(out_bank[:, P:TP], ones[:, :], dg[:, P:TP], start=True, stop=True)
                pe.matmul(out_bank[:, TP:N], ones[0:NS, :], dg[0:NS, TP:N], start=True, stop=True).then_inc(signal, 1)

            pe.wait_ge(cst_loaded, 16)
            pe.wait_ge(par_loaded, 16 * len(PARAMS))
            pe.transpose(TK[:, 0:n_par], prow[:, :], ident[0:n_par, 0:n_par]).then_inc(par_t, 1)
            for i in range(3):
                pe.wait_ge(x_loaded[i], 16)
            for k in range(KD):
                b4 = (SA, SB, SC, TV)[k % 4]
                if k >= 4:
                    pe.wait_ge((xres_act, xres_dve)[k % 2], k // 2 - 1)
                pe.transpose(b4[:, 0:P], xt[:, 0, k * P:(k + 1) * P], ident)
                pe.transpose(b4[:, P:TP], xt[:, 1, k * P:(k + 1) * P], ident)
                pe.transpose(b4[:, TP:N], xt[0:NS, 2, k * P:(k + 1) * P], ident[0:NS, 0:NS]).then_inc(xt_t, 1)

            def x_tile(k):
                pe.wait_ge(ahi_ready, k + 1)
                pe.wait_ge(alo_ready, k + 1)

            def rms_first():
                pe.wait_ge(fill_done, 3)
                pe.wait_ge(rms_diag, 1)
                to_all(TK, rms_bcast)

            def cache_tiles(g):
                pe.wait_ge(cache_loaded, 16)
                after(pe, cache_in, g)
                for c in range(2):
                    cols = slice((2 * g + c) * P, (2 * g + c + 1) * P)
                    last = pe.transpose(OT[:, c * P:c * P + NB * CACHE], cache_t[:, cols],
                                        ident[0:NB * CACHE, 0:NB * CACHE])
                last.then_inc(cache_tr, 1)

            def pool_states(g):
                pe.wait_ge(tails_ready, g + 1)
                after(pe, st_copied, g)
                for c in range(2):
                    pe.transpose(TK[0:NB * CACHE, c * P:(c + 1) * P], tails[:, c, 0:NB * CACHE], ident)
                    last = pe.transpose(TK[0:CACHE, TP + c * P:TP + (c + 1) * P], tails[:, c, NB * CACHE:], ident)
                last.then_inc(st_tr, 1)

            def pool_product(g):
                pe.wait_ge(wp_loaded, 16)
                pe.wait_ge(pooled_ready, g + 1)
                for ct, bk in enumerate((SA, SB)):
                    if g >= 1:
                        pe.wait_ge(mp_lo_s, 2 * (g - 1) + ct + 1)
                    for kc in range(2):
                        last = pe.matmul(bk[:, 0:N], wp[:, g, kc, ct * P:(ct + 1) * P], pooled[:, kc, :],
                                         start=(kc == 0), stop=(kc == 1))
                    last.then_inc(pool_mm, 1)

            for g in range(NG):
                def first(g=g):
                    cache_tiles(g)
                    if g >= 1:
                        pool_states(g - 1)

                def third(g=g):
                    if g >= 1:
                        pool_product(g - 1)
                unit(U0 + 2 * g, 0, a_rhs, between=(first, rms_first if g == 0 else None),
                     tile_wait=x_tile if g == 0 else None)
                unit(U0 + 2 * g + 1, 1, a_rhs, between=(None, third))

            def rec_scores(r):
                pe.wait_ge(unit_read, H0 + 3 * r + 3)
                after(pe, ostd, r)
                for i, (t0, t1) in enumerate(((0, P), (P, TP), (TP, N))):
                    last = pe.transpose(TV[0:t1 - t0, i * P:(i + 1) * P], vv[:, t0:t1], ident)
                last.then_inc(v_tr, 1)
                pe.wait_ge(kx_ready, (LP + 1) * (r + 1))
                after(pe, kt_ready, r)
                pe.transpose(TK[:, 0:P], kx[LP][:, 0:P], ident)
                pe.transpose(TK[:, P:TP], kx[LP][:, P:TP], ident)
                pe.transpose(TK[0:NS, TP:TP + P], kx[LS][:, TP:N], ident).then_inc(k_tr, 1)
                pe.wait_ge(q_ready, r + 1)
                pe.wait_ge(qr_ready, (LP + 1) * (r + 1))
                after(pe, s2_ready, r)
                after(pe, sn_ready, r)

                def level(bk, at, l):
                    for c in range(NC):
                        last = pe.matmul(bk[:, at + c * 64:at + c * 64 + 64].rearrange("p (m j) -> p m j", j=2 ** l),
                                         kx[l][:, c * CH:(c + 1) * CH], right_half(qr[l][:, c * CH:(c + 1) * CH], l),
                                         start=True, stop=True)
                    return last
                for l in range(4, LP):
                    last = level(SC, (l - 4) * P, l)
                last.then_inc(sc_mm, 1)
                for c in range(NC):
                    pe.matmul(SA[:, c * CH:(c + 1) * CH], kx[0][:, c * CH:(c + 1) * CH], qq[:, c * CH:(c + 1) * CH],
                              start=True, stop=True)
                last = pe.matmul(SA[0:NS, TP:N], kx[0][:, TP:N], qq[:, TP:N], start=True, stop=True)
                for l in range(LS):
                    last = pe.matmul(SA[0:NS, N + 32 * l:N + 32 * l + 32].rearrange("p (m j) -> p m j", j=2 ** l),
                                     kx[l][:, TP:N], right_half(qr[l][:, TP:N], l), start=True, stop=True)
                last.then_inc(sc_mm, 1)
                for l in range(4):
                    last = level(SB, l * P, l)
                last.then_inc(sc_mm, 1)

            def rec_state(r):
                pe.wait_ge(vt_ready, r + 1)
                pe.wait_ge(kt_ready, r + 1)
                pe.wait_ge(sc_put, PUTS * r + LP - 4)
                for c in range(NC):
                    last = pe.matmul(SC[:, c * P:(c + 1) * P], kt[:, c, :], vt[:, c, :], start=True, stop=True)
                last.then_inc(st_mm, 1)

            def rec_out(r):
                pe.wait_ge(s0_loaded, 16 * (r + 1))
                pe.wait_ge(s1_ready, r + 1)
                pe.wait_ge(sc_put, PUTS * (r + 1))
                after(pe, on_ready, r)
                pe.matmul(OT[:, 0:CH], vt[:, 0, :], sc[:, 0, :], start=True, stop=False)
                pe.matmul(OT[:, CH:TP], vt[:, 1, :], sc[:, 1, :], start=False, stop=False)
                pe.matmul(OT[:, CH:TP], s1[:, :], qr[LP][:, CH:TP], start=False, stop=False)
                pe.matmul(OT[:, TP:N], vt[0:NS, 2, :], scs[:, :], start=False, stop=False)
                for b in range(NB):
                    t = slice(TP + b * TS, TP + (b + 1) * TS)
                    last = pe.matmul(OT[:, t], s0[:, b, :], qr[LS][:, t], start=False, stop=(b == NB - 1))
                last.then_inc(o_mm, 1)
                pe.wait_ge(vm_ready, r + 1)
                for i, bk in enumerate((SA, SB)):
                    last = pe.matmul(bk[:, :].rearrange("p (b v) -> p b v", v=P), kt[0:NS, 2, :],
                                     vm[:, 4 * i:4 * i + 4, :], start=True, stop=True)
                last.then_inc(sn_mm, 1)

            def rec_stat(r):
                pe.wait_ge(o_read, 2 * (r + 1))
                token_stats(TV, osq, 1, ostat_mm)

            def rec_bcast(r):
                pe.wait_ge(odiag, r + 1)
                to_all(OT, obc_mm)

            def window(n, par_, r, extra=(None, None)):
                def at(f):
                    return (lambda: f(r)) if r is not None else None
                unit(n, par_, a_rhs, between=(at(rec_scores) if r is not None else extra[0], at(rec_state)))
                unit(n + 1, 1 - par_, a_rhs, between=(at(rec_out), at(rec_stat) if r is not None else extra[1]))
                unit(n + 2, par_, a_rhs, between=(None, at(rec_bcast)))

            window(H0, 0, None, (lambda: pool_states(NG - 1), lambda: pool_product(NG - 1)))
            window(H0 + 3, 1, 0)
            with pe.Fori(0, (HEADS - 2) // 2) as i:
                window(H0 + 6 + 6 * i, 0, 2 * i + 1)
                window(H0 + 9 + 6 * i, 1, 2 * i + 2)
            window(G0, 0, HEADS - 1)
            unit(G0 + 3, 1, a_rhs)
            with pe.Fori(0, (HEADS - 4) // 2) as i:
                for k in range(2):
                    unit(G0 + 4 + 2 * i + k, k, a_rhs)

            def m_tile(k):
                if k == 0:
                    pe.wait_ge(mp_lo_s, HEADS)
                if k >= HEADS:
                    pe.wait_ge(gm_hi, k - HEADS + 1)
                    pe.wait_ge(gm_lo, k - HEADS + 1)
            unit(O0, 0, m_rhs, tile_wait=m_tile)
            unit(O0 + 1, 1, m_rhs)
            with pe.Fori(1, KD // 2) as i:
                for k in range(2):
                    unit(O0 + 2 * i + k, k, m_rhs)

            def a2_tile(k):
                pe.wait_ge(h2_hi, k + 1)
                pe.wait_ge(h2_lo, k + 1)

            def rms_second():
                pe.wait_ge(x1_acc, KD)
                token_stats(TV, acc, 0, stat_mm)

            def rms_second_all():
                pe.wait_ge(rms_diag, 2)
                to_all(TK, rms_bcast)

            def ffn(b, first, final):
                n0 = F0 + PER_BLOCK * b
                if first:
                    unit(n0, 0, a_rhs, between=(rms_second, rms_second_all), tile_wait=a2_tile)
                    unit(n0 + 1, 1, a_rhs)
                with pe.Fori(1 if first else 0, KB) as j:
                    unit(n0 + 2 * j, 0, a_rhs)
                    unit(n0 + 2 * j + 1, 1, a_rhs)
                nd = n0 + 2 * KB

                def h_tile(k):
                    pe.wait_ge(hid_hi, KB * b + k + 1)
                    pe.wait_ge(hid_lo, KB * b + k + 1)

                def y_tiles(j, par_):
                    def go():
                        pe.wait_ge(x2_scaled, j + 1)
                        after(pe, y_copied, j - 1)
                        bk = (SA, SB)[par_]
                        for i, (t0, t1) in enumerate(((0, P), (P, TP), (TP, N))):
                            last = pe.transpose(bk[0:t1 - t0, i * P:(i + 1) * P], x2g[:, par_, t0:t1], ident)
                        last.then_inc(y_tr, 1)
                    return go

                unit(nd, 0, h_rhs, HALF_D, tile_wait=h_tile)
                unit(nd + 1, 1, h_rhs, HALF_D, between=(None, y_tiles(0, 0) if final else None))
                if final:
                    for k in range(2):
                        unit(nd + 2 + k, k, h_rhs, HALF_D, between=(None, y_tiles(1 + k, 1 - k)))
                with pe.Fori(2 if final else 1, KD // 2) as j:
                    for k in range(2):
                        unit(nd + 2 * j + k, k, h_rhs, HALF_D,
                             between=(None, y_tiles(2 * j + k - 1, 1 - k) if final else None))
                if final:
                    y_tiles(KD - 1, 1)()

            ffn(0, True, False)
            with pe.Fori(1, BLOCKS - 1) as b:
                ffn(b, False, False)
            ffn(BLOCKS - 1, False, True)
            pe.wait_ge(x2_acc, KD)
            token_stats(TV, acc, 0, stat_mm)

        @block.scalar
        def _(act):
            def split_hi(n, par_, halves=HALF):
                act.wait_ge(raw_loaded[par_], 8 * (n - par_) + 16)
                for p, (k0, k1) in enumerate(halves):
                    after(act, piece_used, 2 * n + p - 3)
                    act.activation(whi[:, par_, k0 * P:k1 * P], raw[:, par_, k0 * P:k1 * P], ACT.Copy)\
                       .then_inc(hi_ready, 1)

            load_params(act, PARAMS[3:])
            act.dma_start(xt[:, 1, :], x_prompt[0, P:TP, :]).then_inc(x_loaded[1], 16)
            act.dma_start(xt[0:NS, 2, :], x_sample.rearrange("b t d -> (b t) d")).then_inc(x_loaded[2], 16)
            act.wait_ge(lb_max, 1)
            act.activation(lbt[:, 1:3, :], lbt[:, 1:3, :], ACT.Exp).then_inc(lb_exp, 1)
            act.wait_ge(fill_done, 3)

            def squares(i):
                rows = P if i < 2 else NS
                act.wait_ge(x_loaded[i], 16)
                for half in range(2):
                    after(act, ss_ready, 2 * i + half)
                    act.activation(junk[0:rows, :], xt[0:rows, i, half * 1024:(half + 1) * 1024], ACT.Square,
                                   accum_out=stat[0:rows, 2 * i + half:2 * i + half + 1]).then_inc(ss_ready, 1)

            squares(0)
            act.wait_ge(par_ready, 1)
            for k in range(KD + 2):
                if k < KD and k % 2 == 0:
                    act.wait_ge(xt_t, k + 1)
                    act.activation(x1[:, k, :], (SA, SB, SC, TV)[k % 4][:, 0:N], ACT.Copy).then_inc(xres_act, 1)
                if k >= 2:
                    q = k - 2
                    act.wait_ge((xres_act, xres_dve)[q % 2], q // 2 + 1)
                    act.activation(a_hi[:, q, :], x1[:, q, :], ACT.Copy, scale=pcol("norm1", q)).then_inc(ahi_ready, 1)
                if k == 3:
                    split_hi(0, 0)
            squares(1)
            squares(2)
            act.wait_ge(ss_ready, 7)
            act.activation(stat[:, 9:12], stat[:, 6:9], ACT.Sqrt, bias=epst[:, 0:1], scale=1.0 / D).then_inc(rms_std, 1)

            def cache_copy(g):
                act.wait_ge(cache_tr, g + 1)
                after(act, pooled_ready, g - 1)
                act.wait_ge(pad_zero, 1)
                for c in range(2):
                    seqs = uu[:, g % 2, c, CACHE + TP:UW].rearrange("p (b t) -> p b t", b=NB)[:, :, 0:CACHE]
                    last = act.activation(seqs, OT[:, c * P:c * P + NB * CACHE].rearrange("p (b t) -> p b t", b=NB),
                                          ACT.Copy)
                last.then_inc(cache_in, 1)

            def tail_copy(g):
                act.wait_ge(unit_read, U0 + 2 * g + 2)
                after(act, st_tr, g)
                for c in range(2):
                    row = uu[:, g % 2, c, :]
                    act.activation(tails[:, c, 0:NB * CACHE].rearrange("p (b t) -> p b t", b=NB),
                                   row[:, CACHE + TP:UW].rearrange("p (b t) -> p b t", b=NB)[:, :, TS:TS + CACHE],
                                   ACT.Copy)
                    last = act.activation(tails[:, c, NB * CACHE:], row[:, TP:TP + CACHE], ACT.Copy)
                last.then_inc(tails_ready, 1)

            def state_copy(g):
                act.wait_ge(st_tr, g + 1)
                act.activation(st_s[:, g * TP:(g + 1) * TP], TK[0:NB * CACHE, 0:TP], ACT.Copy)
                act.activation(st_p[:, g * TP:(g + 1) * TP], TK[0:CACHE, TP:2 * TP], ACT.Copy).then_inc(st_copied, 1)

            def pool_hi(g):
                for ct, bk in enumerate((SA, SB)):
                    j = 2 * g + ct
                    act.wait_ge(pool_mm, j + 1)
                    act.activation(bp_hi[:, j, :], bk[:, 0:N], ACT.Copy, scale=pcol("pool_scale", j)).then_inc(mp_hi_s, 1)

            for g in range(NG):
                split_hi(U0 + 2 * g + 1, 1)
                if g >= 1:
                    tail_copy(g - 1)
                cache_copy(g)
                if g >= 1:
                    state_copy(g - 1)
                split_hi(U0 + 2 * g + 2, 0)
                if g >= 1:
                    pool_hi(g - 1)

            def forget(h):
                act.wait_ge(unit_read, H0 + 3 * h + 1)
                after(act, q_ready, h)
                act.activation(sgm[:, :], zf[:, :], ACT.Sigmoid).then_inc(zf_sig, 1)
                after(act, kx_ready, (LP + 1) * h)
                after(act, qr_ready, (LP + 1) * h)
                act.wait_ge(zf_sig, h + 1)
                act.activation(tl[0][:, :, 1:3], sgm[:, :].rearrange("p (m a) -> p m a", a=2), ACT.Identity,
                               bias=lbt[:, 4, bass.ds(h, 1)], scale=lbt[:, 5, bass.ds(h, 1)]).then_inc(f_ready, 1)

            def sigmoid_q(h):
                act.wait_ge(unit_read, H0 + 3 * h + 2)
                act.wait_ge(f_ready, h + 1)
                act.activation(sgm[:, :], zq[:, :], ACT.Sigmoid).then_inc(zq_sig, 1)

            def rec_tokens(r):
                act.wait_ge(v_tr, r + 1)
                after(act, sn_mm, r)
                act.activation(vt[:, 0:2, :], TV[:, 0:TP].rearrange("p (c v) -> p c v", c=2), ACT.Copy)
                act.activation(vt[0:NS, 2, :], TV[0:NS, TP:TP + P], ACT.Copy).then_inc(vt_ready, 1)
                act.wait_ge(k_tr, r + 1)
                act.activation(kt[:, 0:2, :], TK[:, 0:TP].rearrange("p (c v) -> p c v", c=2), ACT.Copy)
                act.activation(kt[0:NS, 2, :], TK[0:NS, TP:TP + P], ACT.Copy).then_inc(kt_ready, 1)

            def rec_squares(r):
                act.wait_ge(o_mm, r + 1)
                after(act, on_ready, r)
                act.activation(osq[:, :], OT[:, 0:N], ACT.Square).then_inc(o_read, 1)
                act.activation(osb[:, :], OT[:, 0:N], ACT.Copy).then_inc(o_read, 1)

            def load_s0(h):
                act.wait_ge(o_mm, h)
                act.wait_ge(sdec_ready, h)
                act.dma_start(s0[:, :, :], state_hgrn[0, :, bass.ds(h, 1), :, :].rearrange("b o k v -> k (b o) v"))\
                   .then_inc(s0_loaded, 16)

            def rec_stores(r):
                act.wait_ge(s2_ready, r + 1)
                act.dma_start(hgrn_prompt[0, 0, bass.ds(r, 1), :, :].rearrange("o k v -> k (o v)"), s2[:, :])\
                   .then_inc(s2_stored, 16)
                act.wait_ge(sn_ready, r + 1)
                act.dma_start(hgrn_sample[0, :, bass.ds(r, 1), :, :].rearrange("b o k v -> k (b o) v"), sn[:, :, :])\
                   .then_inc(sn_stored, 16)

            def rec_std(r):
                act.wait_ge(ostat_mm, r + 1)
                after(act, odiag, r)
                act.activation(stat[:, 6:8], TV[:, 0:2], ACT.Identity, bias=epst[:, 0:1])
                act.activation(stat[0:NS, 8:9], TV[0:NS, 2:3], ACT.Identity, bias=epst[0:NS, 0:1])
                act.activation(stat[:, 0:2], TV[:, 0:2], ACT.Sqrt, bias=epst[:, 0:1])
                act.activation(stat[0:NS, 2:3], TV[0:NS, 2:3], ACT.Sqrt, bias=epst[0:NS, 0:1]).then_inc(ostd, 1)

            def rec_hi(r):
                act.wait_ge(on_ready, r + 1)
                act.activation(bh_hi[:, r, :], on[:, :], ACT.Copy).then_inc(mh_hi_s, 1)

            def gate(h):
                act.wait_ge(unit_read, G0 + h + 1)
                act.activation(sgm[:, :], zf[:, :], ACT.Sigmoid).then_inc(g_sig, 1)
                act.wait_ge(gated, h + 1)
                act.activation(bh_hi[:, h, :], go[:, :], ACT.Copy).then_inc(gm_hi, 1)

            def window(n, par_, h, r):
                split_hi(n + 1, 1 - par_)
                rec_tokens(r)
                forget(h) if h is not None else gate(0)
                split_hi(n + 2, par_)
                rec_squares(r)
                if h is not None:
                    load_s0(r + 1)
                rec_stores(r)
                sigmoid_q(h) if h is not None else gate(1)
                split_hi(n + 3, 1 - par_)
                rec_std(r)
                if h is None:
                    gate(2)
                rec_hi(r)

            split_hi(H0 + 1, 1)
            tail_copy(NG - 1)
            state_copy(NG - 1)
            act.wait_ge(st_copied, NG)
            act.dma_start(pool_sample[0].rearrange("b t c -> (b t) c"), st_s[:, :]).then_inc(out_done, 16)
            act.dma_start(pool_prompt[0, 0], st_p[:, :]).then_inc(out_done, 16)
            act.wait_ge(t_ones, 1)
            forget(0)
            split_hi(H0 + 2, 0)
            sigmoid_q(0)
            split_hi(H0 + 3, 1)
            pool_hi(NG - 1)
            act.wait_ge(sc_zero, 1)
            act.dma_start(s0[:, :, :], state_hgrn[0, :, 0, :, :].rearrange("b k v -> k b v")).then_inc(s0_loaded, 16)
            window(H0 + 3, 1, 1, 0)
            with act.Fori(0, (HEADS - 2) // 2) as i:
                window(H0 + 6 + 6 * i, 0, 2 * i + 2, 2 * i + 1)
                window(H0 + 9 + 6 * i, 1, 2 * i + 3, 2 * i + 2)
            act.wait_ge(out_done, 32)
            window(G0, 0, None, HEADS - 1)
            split_hi(G0 + 4, 0)
            gate(3)
            with act.Fori(0, (HEADS - 4) // 2) as i:
                for k in range(2):
                    split_hi(G0 + 5 + 2 * i + k, 1 - k)
                    gate(4 + 2 * i + k)

            def h2_part(j):
                act.wait_ge(unit_read, O0 + j + 1)
                act.activation(a_hi[:, j, :], x1[:, j, :], ACT.Copy, scale=pcol("norm2", j)).then_inc(h2_hi, 1)

            with act.Fori(0, KD // 2) as i:
                for k in range(2):
                    split_hi(O0 + 1 + 2 * i + k, 1 - k)
                    h2_part(2 * i + k)

            def silu(n):
                act.wait_ge(unit_read, n + 1)
                act.activation(sg[:, :], zg[:, :], ACT.Silu).then_inc(gate_act, 1)

            def hidden_hi(c, j):
                act.wait_ge(hid_ready, c + 1)
                act.activation(h_hi[:, j, :], hid[:, :], ACT.Copy).then_inc(hid_hi, 1)

            def ffn(b, first, final):
                n0 = F0 + PER_BLOCK * b

                def pair(j, halves):
                    split_hi(n0 + 2 * j + 1, 1)
                    silu(n0 + 2 * j)
                    split_hi(n0 + 2 * j + 2, 0, halves)
                    hidden_hi(KB * b + j, j)
                if first:
                    split_hi(n0 + 1, 1)
                    act.wait_ge(stat_mm, 1)
                    act.activation(stat[:, 6:8], TV[:, 0:2], ACT.Identity, bias=epst[:, 0:1])
                    act.activation(stat[0:NS, 8:9], TV[0:NS, 2:3], ACT.Identity, bias=epst[0:NS, 0:1])
                    act.activation(stat[:, 0:2], TV[:, 0:2], ACT.Sqrt, bias=epst[:, 0:1])
                    act.activation(stat[0:NS, 2:3], TV[0:NS, 2:3], ACT.Sqrt, bias=epst[0:NS, 0:1]).then_inc(rms_std, 1)
                    silu(n0)
                    split_hi(n0 + 2, 0)
                    hidden_hi(0, 0)
                with act.Fori(1 if first else 0, KB - 1) as j:
                    pair(j, HALF)
                pair(KB - 1, HALF_D)
                nd = n0 + 2 * KB

                def y_part(j, par_):
                    act.wait_ge(unit_read, nd + j + 1)
                    after(act, y_tr, j - 1)
                    act.activation(x2g[:, par_, :], x2[:, par_, :], ACT.Copy, scale=pcol("norm_f", j))\
                       .then_inc(x2_scaled, 1)

                def y_copy(j, par_):
                    act.wait_ge(y_tr, j + 1)
                    bk = (SA, SB)[par_]
                    act.activation(yt[:, 0:2, bass.ds(j * P, P)], bk[:, 0:TP].rearrange("p (c v) -> p c v", c=2),
                                   ACT.Copy)
                    act.activation(yt[0:NS, 2, bass.ds(j * P, P)], bk[0:NS, TP:TP + P], ACT.Copy).then_inc(y_copied, 1)

                if not final:
                    with act.Fori(0, KD // 2 - 1) as j:
                        split_hi(nd + 2 * j + 1, 1, HALF_D)
                        split_hi(nd + 2 * j + 2, 0, HALF_D)
                    split_hi(nd + KD - 1, 1, HALF_D)
                    split_hi(nd + KD, 0)
                else:
                    split_hi(nd + 1, 1, HALF_D)
                    y_part(0, 0)
                    split_hi(nd + 2, 0, HALF_D)
                    y_part(1, 1)
                    y_copy(0, 0)
                    with act.Fori(1, KD // 2 - 1) as j:
                        split_hi(nd + 2 * j + 1, 1, HALF_D)
                        y_part(2 * j, 0)
                        y_copy(2 * j - 1, 1)
                        split_hi(nd + 2 * j + 2, 0, HALF_D)
                        y_part(2 * j + 1, 1)
                        y_copy(2 * j, 0)
                    split_hi(nd + KD - 1, 1, HALF_D)
                    y_part(KD - 2, 0)
                    y_copy(KD - 3, 1)
                    y_part(KD - 1, 1)
                    y_copy(KD - 2, 0)
                    y_copy(KD - 1, 1)

            ffn(0, True, False)
            with act.Fori(1, BLOCKS - 1) as b:
                ffn(b, False, False)
            ffn(BLOCKS - 1, False, True)
            act.wait_ge(stat_mm, 2)
            act.activation(stat[:, 6:8], TV[:, 0:2], ACT.Identity, bias=epst[:, 0:1])
            act.activation(stat[0:NS, 8:9], TV[0:NS, 2:3], ACT.Identity, bias=epst[0:NS, 0:1])
            act.activation(stat[:, 0:2], TV[:, 0:2], ACT.Sqrt, bias=epst[:, 0:1])
            act.activation(stat[0:NS, 2:3], TV[0:NS, 2:3], ACT.Sqrt, bias=epst[0:NS, 0:1]).then_inc(rms_std, 1)
            act.wait_ge(y_rec, 2)
            act.wait_ge(y_copied, KD)
            for i, half in ((0, 0), (1, 0)):
                act.activation(yt[:, i, 0:1024], yt[:, i, 0:1024], ACT.Copy, scale=stat[:, 9 + i:10 + i])\
                   .then_inc(y_scaled_a, 1)
                act.wait_ge(y_scaled_a, i + 1)
                act.dma_start(y_prompt[0, i * P:(i + 1) * P, 0:1024], yt[:, i, 0:1024]).then_inc(out_done, 16)
            for i in range(2):
                act.wait_ge(y_scaled_v, i + 1)
                act.dma_start(y_prompt[0, i * P:(i + 1) * P, 1024:D], yt[:, i, 1024:D]).then_inc(out_done, 16)
            act.wait_ge(y_scaled_v, 3)
            act.dma_start(y_sample.rearrange("b t d -> (b t) d"), yt[0:NS, 2, :]).then_inc(out_done, 16)

        @block.vector
        def _(dve):
            links = [0]

            def link(ins):
                links[0] += 1
                ins.then_inc(dve_link, 1)
                dve.wait_ge(dve_link, links[0])

            def split_lo(n, par_, halves=HALF):
                for p, (k0, k1) in enumerate(halves):
                    dve.wait_ge(hi_ready, 2 * n + p + 1)
                    cols = slice(k0 * P, k1 * P)
                    dve.tensor_tensor(wlo[:, par_, cols], raw[:, par_, cols], whi[:, par_, cols].bitcast(F32), SUB)\
                       .then_inc(lo_ready, 1)

            def done(n):
                dve.wait_ge(piece_used, 2 * n + 2)

            def scaled(n, par_, out):
                done(n)
                return dve.tensor_tensor(out, zb[par_][:, 0:N], rbc[:, :], MUL)

            def split_rest(out_lo, src, out_hi):
                return dve.tensor_tensor(out_lo, src, out_hi.bitcast(F32), SUB)

            dve.memset(ones[:, :], 1.0).then_inc(fill_done, 1)
            dve.memset(meanc[:, 0:1], 1.0 / D)
            dve.memset(meanc[:, 1:2], 1.0 / P)
            dve.memset(epst[:, :], EPS).then_inc(fill_done, 1)
            dve.memset(stat[:, :], 0.5).then_inc(fill_done, 1)
            dve.wait_ge(par_t, 1)
            dve.tensor_copy(par[:, :], TK[:, 0:n_par]).then_inc(par_ready, 1)
            dve.wait_ge(par_ready, 1)
            lb0 = 3 * KD
            rows = par[:, lb0:lb0 + 2 * HEADS].rearrange("p (r h) -> p r h", r=2)
            link(dve.tensor_tensor(lbt[:, 0, :], rows[:, 0, :], rows[:, 1, :], ALU.max))
            dve.tensor_tensor(lbt[:, 1, :], rows[:, 0, :], lbt[:, 0, :], SUB)
            dve.tensor_tensor(lbt[:, 2, :], rows[:, 1, :], lbt[:, 0, :], SUB).then_inc(lb_max, 1)
            dve.wait_ge(lb_exp, 1)
            link(dve.tensor_tensor(lbt[:, 3, :], lbt[:, 1, :], lbt[:, 2, :], ADD))
            link(dve.reciprocal(lbt[:, 0, :], lbt[:, 3, :]))
            link(dve.tensor_tensor(lbt[:, 4, :], lbt[:, 1, :], lbt[:, 0, :], MUL))
            dve.tensor_scalar(lbt[:, 5, :], lbt[:, 4, :], -1.0, 1.0, MUL, ADD).then_inc(lb_ready, 1)
            for k in range(KD + 3):
                if k < KD and k % 2 == 1:
                    dve.wait_ge(xt_t, k + 1)
                    dve.tensor_copy(x1[:, k, :], (SA, SB, SC, TV)[k % 4][:, 0:N]).then_inc(xres_dve, 1)
                if k >= 3:
                    q = k - 3
                    dve.wait_ge(ahi_ready, q + 1)
                    dve.scalar_tensor_tensor(out=a_lo[:, q, :], in0=x1[:, q, :], scalar=pcol("norm1", q),
                                             in1=a_hi[:, q, :].bitcast(F32), op0=MUL, op1=SUB).then_inc(alo_ready, 1)
                if k == 4:
                    split_lo(0, 0)
            dve.wait_ge(ss_ready, 6)
            ss = stat[:, 0:6].rearrange("p (i h) -> p i h", h=2)
            dve.tensor_tensor(stat[:, 6:9], ss[:, :, 0], ss[:, :, 1], ADD).then_inc(ss_ready, 1)

            def newton(y, mean, tmp):
                def step(ins):
                    newtons[0] = newtons[0] + 1
                    ins.then_inc(newton_step, 1)
                    dve.wait_ge(newton_step, newtons[0])
                step(dve.tensor_tensor(tmp, y, y, MUL))
                step(dve.tensor_tensor(tmp, tmp, mean, MUL))
                step(dve.tensor_scalar(tmp, tmp, -0.5, 1.5, MUL, ADD))
                step(dve.tensor_tensor(y, y, tmp, MUL))

            def diagonals(src, signal):
                dve.tensor_tensor(dg[:, 0:TP].rearrange("p (c t) -> p c t", c=2),
                                  ident.unsqueeze(1).to_broadcast([P, 2, P]),
                                  stat[:, src:src + 2].unsqueeze(2).to_broadcast([P, 2, P]), MUL)
                dve.tensor_scalar(dg[0:NS, TP:N], ident[0:NS, 0:NS], stat[0:NS, src + 2:src + 3], None, MUL)\
                   .then_inc(signal, 1)

            def rms_row(count):
                dve.wait_ge(rms_bcast, count)
                dve.tensor_copy(rbc[:, :], TK[:, 0:N]).then_inc(rms_ready, 1)
                dve.wait_ge(rms_ready, count)

            dve.wait_ge(rms_std, 1)
            link(dve.tensor_scalar(stat[:, 3:6], stat[:, 6:9], 1.0 / D, EPS, MUL, ADD))
            link(dve.reciprocal(stat[:, 6:9], stat[:, 9:12]))
            newtons = [0]
            newton(stat[:, 6:9], stat[:, 3:6], stat[:, 0:3])
            diagonals(6, rms_diag)

            dve.wait_ge(pad_zero, 1)

            def u_part(ft):
                g, c = ft // 2, ft % 2
                done(U0 + ft)
                after(dve, pooled_ready, g - 1)
                after(dve, tails_ready, g - 1)
                row = uu[:, g % 2, c, :]
                dve.tensor_tensor(row[:, CACHE:CACHE + TP], zb[c][:, 0:TP], rbc[:, 0:TP], MUL)
                dve.tensor_tensor(row[:, CACHE + TP:UW].rearrange("p (b t) -> p b t", b=NB)[:, :, CACHE:CACHE + TS],
                                  zb[c][:, TP:N].rearrange("p (b t) -> p b t", b=NB),
                                  rbc[:, TP:N].rearrange("p (b t) -> p b t", b=NB), MUL).then_inc(unit_read, 1)

            def pool_means(g):
                win = (wa, wb, wa, wb)[g]
                inv = 1.0 / WINDOWS[g]
                dve.wait_ge(win_ready, g + 1)
                after(dve, pool_mm, 2 * g)
                dve.tensor_tensor(pooled[:, :, 0:16], win[:, :, CACHE:CACHE + 16],
                                  cst[:, C_IC + 16 * g:C_IC + 16 * g + 16].unsqueeze(1).to_broadcast([P, 2, 16]),
                                  MUL).then_inc(fix_ready, 1)
                for c in range(2):
                    def seqs(ap):
                        return ap[:, c, CACHE + TP:UW].rearrange("p (b t) -> p b t", b=NB)[:, :, CACHE:CACHE + TS]
                    dve.scalar_tensor_tensor(out=pooled[:, c, TP:N].rearrange("p (b t) -> p b t", b=NB),
                                             in0=seqs(win), scalar=inv, in1=seqs(uu[:, g % 2]), op0=MUL, op1=SUB)
                dve.scalar_tensor_tensor(out=pooled[:, :, 16:TP], in0=win[:, :, CACHE + 16:CACHE + TP], scalar=inv,
                                         in1=uu[:, g % 2, :, CACHE + 16:CACHE + TP], op0=MUL, op1=SUB)
                dve.wait_ge(fix_ready, g + 1)
                dve.tensor_tensor(pooled[:, :, 0:16], pooled[:, :, 0:16], uu[:, g % 2, :, CACHE:CACHE + 16], SUB)\
                   .then_inc(pooled_ready, 1)

            def pool_lo(g):
                for ct, bk in enumerate((SA, SB)):
                    j = 2 * g + ct
                    dve.wait_ge(mp_hi_s, j + 1)
                    dve.scalar_tensor_tensor(out=bp_lo[:, j, :], in0=bk[:, 0:N], scalar=pcol("pool_scale", j),
                                             in1=bp_hi[:, j, :].bitcast(F32), op0=MUL, op1=SUB).then_inc(mp_lo_s, 1)

            for g in range(NG):
                split_lo(U0 + 2 * g + 1, 1)
                if g >= 1:
                    pool_means(g - 1)
                if g == 0:
                    rms_row(1)
                u_part(2 * g)
                split_lo(U0 + 2 * g + 2, 0)
                if g >= 1:
                    pool_lo(g - 1)
                u_part(2 * g + 1)

            def products(h):
                dve.wait_ge(f_ready, h + 1)
                after(dve, sdec_ready, h)
                after(dve, kx_ready, (LP + 1) * h)
                for l in range(LP):
                    if l:
                        dve.wait_ge(prod_ready, LP * h + l)
                    m = (N if l < LS else TP) // 2 ** (l + 1)
                    dve.tensor_tensor(tl[l + 1][:, 0:m // 2, 1:3], prod_in(l, 1), prod_in(l, 2), MUL)\
                       .then_inc(prod_ready, 1)

            def queries(h):
                dve.wait_ge(q_ready, h + 1)
                after(dve, o_mm, h)
                dve.tensor_tensor(qr[0][:, :].rearrange("p (m a) -> p m a", a=2),
                                  qq[:, :].rearrange("p (m a) -> p m a", a=2), tl[0][:, :, 1:3], MUL)\
                   .then_inc(qr_ready, 1)
                for l in range(LP):
                    n = N if l < LS else TP
                    dve.wait_ge(qr_ready, (LP + 1) * h + l + 1)
                    dve.tensor_tensor(blocks_of(qr[l + 1], l, n), blocks_of(qr[l], l, n), times(l, n, 0), MUL)\
                       .then_inc(qr_ready, 1)

            def mask(col, n, l, rows=P):
                m = cst[0:rows, col:col + n].bitcast(U32)
                return m.rearrange("p (m j) -> p m j", j=2 ** l)

            def rec_scores(r):
                puts = [PUTS * r]

                def put(out, where, src):
                    after(dve, sc_put, puts[0])
                    dve.sem_inc(put_go, 1)
                    dve.copy_predicated(out, where, src).then_inc(sc_put, 1)
                    puts[0] = puts[0] + 1

                def put_level(bk, at_, l):
                    put(right_half(sc[:, :, :].rearrange("p c t -> p (c t)"), l), mask(C_MP + l * P, P, l),
                        bk[:, at_:at_ + P].rearrange("p (m j) -> p m j", j=2 ** l))

                after(dve, o_mm, r)
                dve.wait_ge(sc_mm, 3 * r + 1)
                for l in range(4, LP):
                    put_level(SC, (l - 4) * P, l)
                dve.wait_ge(sc_mm, 3 * r + 2)
                put(sc[:, :, :], ident.bitcast(U32).unsqueeze(1).to_broadcast([P, NC, CH]),
                    SA[:, 0:TP].rearrange("p (c t) -> p c t", c=NC))
                put(scs[:, :], ident[0:NS, 0:NS].bitcast(U32), SA[0:NS, TP:N])
                for l in range(LS):
                    put(right_half(scs[:, :], l), mask(C_MS + 32 * l, 32, l, NS),
                        SA[0:NS, N + 32 * l:N + 32 * l + 32].rearrange("p (m j) -> p m j", j=2 ** l))
                dve.wait_ge(sc_mm, 3 * r + 3)
                for l in range(4):
                    put_level(SB, l * P, l)

            def rec_state(r):
                dve.wait_ge(st_mm, r + 1)
                after(dve, s2_stored, 16 * r)
                dve.tensor_copy(s1[:, :], SC[:, 0:P]).then_inc(s1_ready, 1)
                dve.wait_ge(s1_ready, r + 1)
                dve.scalar_tensor_tensor(out=s2[:, :], in0=s1[:, :], scalar=tl[LP][:, 0, 2:3],
                                         in1=SC[:, P:2 * P], op0=MUL, op1=ADD).then_inc(s2_ready, 1)

            def rec_sample_state(r):
                dve.wait_ge(sn_mm, r + 1)
                dve.wait_ge(sdec_ready, r + 1)
                for i, bk in enumerate((SA, SB)):
                    part = sn[:, 4 * i:4 * i + 4, :]
                    last = dve.tensor_tensor(part, part, bk[:, :].rearrange("p (b v) -> p b v", v=P), ADD)
                last.then_inc(sn_ready, 1)

            def rec_rms(r):
                dve.wait_ge(ostd, r + 1)
                after(dve, obc_mm, r)
                dve.reciprocal(stat[:, 3:6], stat[:, 0:3]).then_inc(orec, 1)
                dve.wait_ge(orec, r + 1)
                newtons[0] = 4 * (r + 1)
                newton(stat[:, 3:6], stat[:, 6:9], stat[:, 9:12])
                diagonals(3, odiag)

            def rec_norm(r):
                dve.wait_ge(obc_mm, r + 1)
                after(dve, mh_hi_s, r)
                dve.scalar_tensor_tensor(out=on[:, :], in0=osb[:, :], scalar=pcol("hg_norm", r), in1=OT[:, 0:N],
                                         op0=MUL, op1=MUL).then_inc(on_ready, 1)

            def rec_lo(r):
                dve.wait_ge(mh_hi_s, r + 1)
                split_rest(bh_lo[:, r, :], on[:, :], bh_hi[:, r, :]).then_inc(mh_lo_s, 1)

            def gate(n, par_, h):
                scaled(n, par_, zf[:, :]).then_inc(unit_read, 1)
                after(dve, gm_lo, h)
                dve.tensor_tensor(go[:, :], bh_hi[:, h, :].bitcast(F32), bh_lo[:, h, :].bitcast(F32), ADD)\
                   .then_inc(osum, 1)
                dve.wait_ge(osum, h + 1)
                dve.wait_ge(g_act, h + 1)
                dve.tensor_tensor(go[:, :], go[:, :], zq[:, :], MUL).then_inc(gated, 1)
                dve.wait_ge(gm_hi, h + 1)
                split_rest(bh_lo[:, h, :], go[:, :], bh_hi[:, h, :]).then_inc(gm_lo, 1)

            def window(n, par_, h, r):
                split_lo(n + 1, 1 - par_)
                if r is not None:
                    rec_scores(r)
                scaled(n, par_, zf[:, :]).then_inc(unit_read, 1) if h is not None else gate(n, par_, 0)
                if r is not None:
                    rec_state(r)
                split_lo(n + 2, par_)
                if r is not None:
                    rec_sample_state(r)
                else:
                    pool_means(NG - 1)
                    dve.wait_ge(t_ones, 1)
                if h is not None:
                    products(h)
                    scaled(n + 1, 1 - par_, zq[:, :]).then_inc(unit_read, 1)
                else:
                    gate(n + 1, 1 - par_, 1)
                split_lo(n + 3, 1 - par_)
                if r is not None:
                    rec_rms(r)
                if h is not None:
                    queries(h)
                if h is not None:
                    if r is None:
                        pool_lo(NG - 1)
                        dve.wait_ge(sc_zero, 1)
                    scaled(n + 2, par_, vv[:, :]).then_inc(unit_read, 1)
                else:
                    gate(n + 2, par_, 2)
                if r is not None:
                    rec_norm(r)
                    rec_lo(r)

            window(H0, 0, 0, None)
            window(H0 + 3, 1, 1, 0)
            with dve.Fori(0, (HEADS - 2) // 2) as i:
                window(H0 + 6 + 6 * i, 0, 2 * i + 2, 2 * i + 1)
                window(H0 + 9 + 6 * i, 1, 2 * i + 3, 2 * i + 2)
            window(G0, 0, None, HEADS - 1)
            split_lo(G0 + 4, 0)
            gate(G0 + 3, 1, 3)
            with dve.Fori(0, (HEADS - 4) // 2) as i:
                for k in range(2):
                    split_lo(G0 + 5 + 2 * i + k, 1 - k)
                    gate(G0 + 4 + 2 * i + k, k, 4 + 2 * i + k)

            with dve.Fori(0, KD // 2) as i:
                for k in range(2):
                    j = 2 * i + k
                    split_lo(O0 + 1 + j, 1 - k)
                    done(O0 + j)
                    dve.tensor_tensor(x1[:, j, :], x1[:, j, :], zb[k][:, 0:N], ADD).then_inc(unit_read, 1)
                    dve.wait_ge(h2_hi, j + 1)
                    dve.scalar_tensor_tensor(out=a_lo[:, j, :], in0=x1[:, j, :], scalar=pcol("norm2", j),
                                             in1=a_hi[:, j, :].bitcast(F32), op0=MUL, op1=SUB).then_inc(h2_lo, 1)

            def ffn(b, first, final):
                n0 = F0 + PER_BLOCK * b

                def up(n, c, j):
                    scaled(n, 1, zu[:, :]).then_inc(unit_read, 1)
                    dve.wait_ge(unit_read, n + 1)
                    dve.wait_ge(gate_act, c + 1)
                    dve.tensor_tensor(hid[:, :], zu[:, :], sg[:, :], MUL).then_inc(hid_ready, 1)
                    dve.wait_ge(hid_hi, c + 1)
                    split_rest(h_lo[:, j, :], hid[:, :], h_hi[:, j, :]).then_inc(hid_lo, 1)

                def pair(j, halves):
                    n = n0 + 2 * j
                    split_lo(n + 1, 1)
                    scaled(n, 0, zg[:, :]).then_inc(unit_read, 1)
                    split_lo(n + 2, 0, halves)
                    up(n + 1, KB * b + j, j)
                if first:
                    split_lo(n0 + 1, 1)
                    dve.wait_ge(rms_std, 2)
                    dve.reciprocal(stat[:, 3:6], stat[:, 0:3]).then_inc(orec, 1)
                    dve.wait_ge(orec, HEADS + 1)
                    newtons[0] = 4 * (HEADS + 1)
                    newton(stat[:, 3:6], stat[:, 6:9], stat[:, 9:12])
                    diagonals(3, rms_diag)
                    rms_row(2)
                    scaled(n0, 0, zg[:, :]).then_inc(unit_read, 1)
                    split_lo(n0 + 2, 0)
                    up(n0 + 1, 0, 0)
                with dve.Fori(1 if first else 0, KB - 1) as j:
                    pair(j, HALF)
                pair(KB - 1, HALF_D)
                nd = n0 + 2 * KB

                def down(j, par_):
                    done(nd + j)
                    if final:
                        after(dve, x2_acc, j - 1)
                        after(dve, x2_scaled, j - 1)
                        dve.tensor_tensor(x2[:, par_, :], x1[:, j, :], zb[par_][:, 0:N], ADD).then_inc(unit_read, 1)
                    else:
                        dve.tensor_tensor(x1[:, j, :], x1[:, j, :], zb[par_][:, 0:N], ADD).then_inc(unit_read, 1)

                def down_pair(j):
                    split_lo(nd + 2 * j + 1, 1, HALF_D)
                    down(2 * j, 0)
                    split_lo(nd + 2 * j + 2, 0, HALF_D)
                    down(2 * j + 1, 1)
                if final:
                    down_pair(0)
                with dve.Fori(1 if final else 0, KD // 2 - 1) as j:
                    down_pair(j)
                split_lo(nd + KD - 1, 1, HALF_D)
                down(KD - 2, 0)
                if not final:
                    split_lo(nd + KD, 0)
                down(KD - 1, 1)

            ffn(0, True, False)
            with dve.Fori(1, BLOCKS - 1) as b:
                ffn(b, False, False)
            ffn(BLOCKS - 1, False, True)
            dve.wait_ge(rms_std, 3)
            dve.reciprocal(stat[:, 3:6], stat[:, 0:3]).then_inc(y_rec, 1)
            dve.wait_ge(y_rec, 1)
            newtons[0] = 4 * (HEADS + 2)
            newton(stat[:, 3:6], stat[:, 6:9], stat[:, 9:12])
            dve.tensor_copy(stat[:, 9:12], stat[:, 3:6]).then_inc(y_rec, 1)
            dve.wait_ge(y_copied, KD)
            for i in range(2):
                dve.tensor_scalar(yt[:, i, 1024:D], yt[:, i, 1024:D], stat[:, 3 + i:4 + i], None, MUL)\
                   .then_inc(y_scaled_v, 1)
            dve.tensor_scalar(yt[0:NS, 2, :], yt[0:NS, 2, :], stat[0:NS, 5:6], None, MUL).then_inc(y_scaled_v, 1)

        @block.gpsimd
        def _(pool):
            pool.wait_ge(ss_ready, 6)
            for q in range(2):
                last = pool.memset(uu[:, q, :, 0:CACHE], 0.0)
            last.then_inc(pad_zero, 1)
            pool.wait_ge(xt_t, KD)
            for l in range(LP + 1):
                last = pool.memset(tl[l][:, :, :], 1.0)
            last.then_inc(t_ones, 1)

            steps = 0
            for g, w in enumerate(WINDOWS):
                pool.wait_ge(unit_read, U0 + 2 * g + 2)
                pool.wait_ge(cache_in, g + 1)
                after(pool, pooled_ready, g)
                src, dst, spare, first = uu[:, g % 2], wa, wb, 1
                span = 1
                while span < w:
                    ins = pool.tensor_tensor(dst[:, :, first:UW], src[:, :, first:UW], src[:, :, first - span:UW - span],
                                             ADD)
                    span *= 2
                    if span < w:
                        ins.then_inc(win_step, 1)
                        steps += 1
                        pool.wait_ge(win_step, steps)
                    else:
                        ins.then_inc(win_ready, 1)
                    src, dst, spare, first = dst, spare, dst, first + span

            def rec_sample(r):
                pool.wait_ge(s0_loaded, 16 * (r + 1))
                pool.wait_ge(prod_ready, LP * (r + 1))
                after(pool, sn_stored, 16 * r)
                decay = tl[LS][:, TP // TS // 2:N // TS // 2, 1:3].unsqueeze(3).to_broadcast([P, NB // 2, 2, P])
                pool.tensor_tensor(sn[:, :, :].rearrange("p (m a) v -> p m a v", a=2),
                                   s0[:, :, :].rearrange("p (m a) v -> p m a v", a=2), decay, MUL).then_inc(sdec_ready, 1)
                pool.wait_ge(vt_ready, r + 1)
                after(pool, sn_mm, r)
                pool.tensor_tensor(vm[:, :, :], vt[0:NS, 2:3, :].to_broadcast([NS, NB, P]),
                                   cst[0:NS, C_BM:C_BM + NB].unsqueeze(2).to_broadcast([NS, NB, P]), MUL)\
                    .then_inc(vm_ready, 1)

            def keys(h):
                pool.wait_ge(f_ready, h + 1)
                after(pool, sc_mm, 3 * h)
                after(pool, k_tr, h)
                pool.tensor_tensor(kx[0][:, :].rearrange("p (m a) -> p m a", a=2),
                                   ones[:, 0:1].unsqueeze(2).to_broadcast([P, N // 2, 2]), tl[0][:, :, 1:3], SUB)\
                    .then_inc(kx_ready, 1)
                for l in range(LP):
                    n = N if l < LS else TP
                    pool.wait_ge(kx_ready, (LP + 1) * h + l + 1)
                    if l:
                        pool.wait_ge(prod_ready, LP * h + l)
                    pool.tensor_tensor(blocks_of(kx[l + 1], l, n), blocks_of(kx[l], l, n), times(l, n, 2), MUL)\
                        .then_inc(kx_ready, 1)

            def query(h):
                pool.wait_ge(zq_sig, h + 1)
                pool.tensor_tensor(qq[:, :], zq[:, :], sgm[:, :], MUL).then_inc(q_ready, 1)

            def window(h, r):
                rec_sample(r)
                keys(h)
                query(h)

            pool.wait_ge(fill_done, 3)
            keys(0)
            query(0)
            pool.wait_ge(pooled_ready, NG)
            pool.wait_ge(st_tr, NG)
            pool.wait_ge(pool_mm, 2 * NG)
            pool.memset(sc[:, :, :], 0.0)
            pool.memset(scs[:, :], 0.0).then_inc(sc_zero, 1)
            window(1, 0)
            with pool.Fori(0, (HEADS - 2) // 2) as i:
                window(2 * i + 2, 2 * i + 1)
                window(2 * i + 3, 2 * i + 2)
            rec_sample(HEADS - 1)

            def gate(h):
                pool.wait_ge(g_sig, h + 1)
                pool.tensor_tensor(zq[:, :], zf[:, :], sgm[:, :], MUL).then_inc(g_act, 1)

            for h in range(2):
                gate(h)
            with pool.Fori(0, (HEADS - 2) // 2) as i:
                for k in range(2):
                    gate(2 + 2 * i + k)

            pool.wait_ge(gm_lo, HEADS)
            pool.wait_ge(mh_lo_s, HEADS)
            pool.memset(acc[:, :], 0.0).then_inc(acc_zero, 1)
            pool.wait_ge(acc_zero, 1)
            with pool.Fori(0, KD) as j:
                pool.wait_ge(unit_read, O0 + j + 1)
                pool.tensor_tensor(sq[:, :], x1[:, j, :], x1[:, j, :], MUL).then_inc(x1_sq, 1)
                pool.wait_ge(x1_sq, j + 1)
                pool.tensor_tensor(acc[:, :], acc[:, :], sq[:, :], ADD).then_inc(x1_acc, 1)
                pool.wait_ge(x1_acc, j + 1)
            pool.wait_ge(stat_mm, 1)
            pool.memset(acc[:, :], 0.0).then_inc(acc_zero, 1)
            pool.wait_ge(acc_zero, 2)
            nd = F0 + PER_BLOCK * (BLOCKS - 1) + 2 * KB
            with pool.Fori(0, KD // 2) as i:
                for k in range(2):
                    j = 2 * i + k
                    pool.wait_ge(unit_read, nd + j + 1)
                    pool.tensor_tensor(sq[:, :], x2[:, k, :], x2[:, k, :], MUL).then_inc(x2_sq, 1)
                    pool.wait_ge(x2_sq, j + 1)
                    pool.tensor_tensor(acc[:, :], acc[:, :], sq[:, :], ADD).then_inc(x2_acc, 1)
                    pool.wait_ge(x2_acc, j + 1)


INS = ["x_prompt", "x_sample", "cache_pool", "state_hgrn", "lb_param", "norm1", "w_in", "w_pool", "pool_scale",
       "hg_norm", "w_o", "norm2", "w_gate", "w_up", "w_down", "norm_f"]
OUTS = [(1, TP, D), (NB, TS, D), (1, 1, CACHE, PW), (1, 1, HEADS, P, P), (1, NB, CACHE, PW), (1, NB, HEADS, P, P)]


def kernel(**inputs):
    import numpy as np
    import concourse.bacc as bacc
    from concourse.bass_utils import run_bass_kernel_spmd as run

    nc = bacc.Bacc("TRN2", target_bir_lowering=False, num_devices=1)
    arrays = {f"in_{name}": np.ascontiguousarray(inputs[name]) for name in INS}
    arrays["in_consts"] = constant_table(np)
    args = [nc.dram_tensor(n, a.shape, mybir.dt.from_np(a.dtype), kind="ExternalInput").ap() for n, a in arrays.items()]
    args += [nc.dram_tensor(f"out_{i}", s, F32, kind="ExternalOutput").ap() for i, s in enumerate(OUTS)]
    hybrid_kernel(nc, *args)
    r = run(nc, [arrays], core_ids=[0])
    return tuple(r.results[0][f"out_{i}"] for i in range(len(OUTS)))
```

```python
from contextlib import ExitStack

import concourse.bass as bass
from concourse import mybir

F32 = mybir.dt.float32
F32R = mybir.dt.float32r
BF16 = mybir.dt.bfloat16
U32 = mybir.dt.uint32
ALU = mybir.AluOpType
ACT = mybir.ActivationFunctionType
MUL, ADD, SUB = ALU.mult, ALU.add, ALU.subtract

P = 128
D = 2048
KD = D // P
HD = D // 2
TP, NB, TS = 256, 8, 8
NS = NB * TS
HB, HS = NB // 2, NS // 2
N = TP + NS
CH = 128
NC = TP // CH
PW = 1024
WINDOWS = (2, 4, 8, 16)
NG = len(WINDOWS)
GC = PW // NG
CACHE = max(WINDOWS) - 1
HEADS = 8
FF = 5632
KF = FF // P
BLOCKS = 4
KB = KF // BLOCKS
EPS = 1e-6
LP, LS = 7, 3

PARAMS = (("norm1", KD), ("norm2", KD), ("norm_f", KD), ("lb_param", 2 * HEADS),
          ("pool_scale", PW // P), ("hg_norm", HEADS))
C_ID = 0
C_MP = C_ID + P
C_MS = C_MP + LP * P
C_BM = C_MS + LS * (NS // 2)
C_IC = C_BM + NB // 2
C_END = C_IC + NG * 16

U0 = 0
H0 = PW // P
G0 = H0 + 3 * HEADS
O0 = G0 + HEADS
F0 = O0 + KD
PER_BLOCK = 2 * KB + KD

PUTS = LP + LS + 2


def constant_table(np):
    c = np.zeros((P, C_END), np.float32)
    c[:, C_ID:C_ID + P] = np.eye(P)
    s = np.arange(P)[:, None]
    for level in range(LP):
        half, size = 2 ** level, 2 ** (level + 1)
        t = np.array([t for t in range(CH) if t % size >= half])[None, :]
        m = ((s // size == t // size) & (s % size < half)).astype(np.float32)
        for ch in range(NC):
            c[:, C_MP + level * P + ch * 64:C_MP + level * P + ch * 64 + 64] = m
        if level < LS:
            c[:NS, C_MS + level * 32:C_MS + level * 32 + 32] = m[:NS, :32]
    for b in range(HB):
        for copy in range(3):
            c[copy * HS + b * TS:copy * HS + (b + 1) * TS, C_BM + b] = 1
    for g, w in enumerate(WINDOWS):
        c[:, C_IC + 16 * g:C_IC + 16 * g + 16] = 1 / np.minimum(np.arange(16) + 1, w).astype(np.float32)
    return c


def hybrid_kernel(nc, x_prompt, x_sample, cache_pool, state_hgrn, lb_param, norm1, w_in, w_pool, pool_scale,
                  hg_norm, w_o, norm2, w_gate, w_up, w_down, norm_f, consts,
                  y_prompt, y_sample, pool_prompt, hgrn_prompt, pool_sample, hgrn_sample):
    param_of = {"norm1": norm1, "norm2": norm2, "norm_f": norm_f, "lb_param": lb_param,
                "pool_scale": pool_scale, "hg_norm": hg_norm}

    def by_rows(w):
        return w.rearrange("(k p) c -> p k c", p=P)

    win_v, wo_v = by_rows(w_in[0]), by_rows(w_o[0])
    wg_v, wu_v, wd_v = by_rows(w_gate[0]), by_rows(w_up[0]), by_rows(w_down[0])

    ctx = ExitStack()
    with ctx:
        def keep(name, shape, dt=F32):
            return ctx.enter_context(nc.sbuf_tensor(name, shape, dt))

        def region(stack, tensors):
            return [stack.enter_context(nc.sbuf_tensor(n, s, d)) for n, s, d in tensors]

        def passing(tensors):
            with ExitStack() as st:
                return region(st, tensors)

        def sem(name):
            return ctx.enter_context(nc.semaphore(name))

        x1 = keep("x_res", [P, KD, N])
        a_hi = keep("a_hi", [P, KD, N], F32R)
        a_lo = keep("a_lo", [P, KD, N], F32R)
        raw = keep("w_raw", [P, 2, KD * P])
        whi = keep("w_hi", [P, 2, KD * P], F32R)
        wlo = keep("w_lo", [P, 2, KD * P], F32R)
        cst = keep("cst", [P, C_END])
        n_par = sum(r for _, r in PARAMS)
        par = keep("par", [P, n_par])
        v_rep = keep("v_rep", [P, 6 * HS])
        prow = v_rep[0:n_par, 0:P]
        ones = keep("ones_mat", [P, P])
        meanc = keep("mean_cols", [P, 2])
        rbc = keep("rms_bc", [P, N])
        stat = keep("stat", [P, 12])
        lbt = keep("lb_tmp", [P, 6, HEADS])
        epst = keep("eps_col", [P, 1])
        warm = keep("sqrt_warm", [P, 2])

        h_hi, h_lo = passing([("h_hi", [P, KB, N], F32R), ("h_lo", [P, KB, N], F32R)])
        bp_hi = keep("mp_hi", [P, HEADS, N], F32R)
        bp_lo = keep("mp_lo", [P, HEADS, N], F32R)
        wp, cache_t, st_s, st_p = passing([
            ("wp", [P, NG, 2, GC], F32), ("cache_t", [NB * CACHE, PW], F32),
            ("st_s", [NB * CACHE, PW], F32), ("st_p", [CACHE, PW], F32)])
        bh_hi = keep("mh_hi", [P, HEADS, N], F32R)
        bh_lo = keep("mh_lo", [P, HEADS, N], F32R)

        xt, = passing([("xt", [P, 3, D], F32)])
        zg, sg, zu, hid, sq, acc, x2, x2g = passing([
            (n, [P, N], F32) for n in ("zg", "sg", "zu", "hid", "sq", "acc")] + [
            ("x2", [P, 2, N], F32), ("x2g", [P, 2, N], F32)])
        with ExitStack() as st:
            region(st, [("pad_ffn", [P, 10 * N], F32)])
            yt, = region(st, [("yt", [P, 3, D], F32)])
        early = ExitStack()
        zf, = region(early, [("zf", [P, N], F32)])
        zq, sgm, qq = region(early, [(n, [P, N], F32) for n in ("zq", "sgm", "qq")])
        tl = region(early, [(f"t{l}", [P, (N if l <= LS else TP) // 2 ** (l + 1), 4], F32) for l in range(LP + 1)])
        qr = region(early, [(f"qr{l}", [P, N if l <= LS else TP], F32) for l in range(LP + 1)])
        kx = region(early, [(f"kx{l}", [P, N if l <= LS else TP], F32) for l in range(LP + 1)])
        junk, = passing([("junk", [P, 1024], BF16)])
        UW = CACHE + TP + NB * (CACHE + TS)
        uu, wa, wb, pooled, tails = passing([
            ("uu", [P, 2, 2, UW], F32), ("wa", [P, 2, UW], F32), ("wb", [P, 2, UW], F32), ("pooled", [P, 2, N], F32),
            ("tails", [P, 2, NB * CACHE + CACHE], F32)])
        late = ExitStack()
        vv, osb, on = region(late, [(n, [P, N], F32) for n in ("vv", "osb", "on")])
        vt, kt = region(late, [("vt", [P, 3, P], F32), ("kt", [P, 2, P], F32)])
        sc, scs = region(late, [("sc", [P, NC, CH], F32), ("scs", [NS, NS], F32)])
        s0, sn = region(late, [("s0", [P, NB, P], F32), ("sn", [P, NB, P], F32)])
        k3, v3 = region(late, [("k3", [3 * HS, 2, P], F32R), ("v3", [3 * HS, 2, P], F32R)])
        vm, = region(late, [("vm", [3 * HS, 2, HB, P], F32R)])
        s1, s2, dg = region(late, [("s1", [P, P], F32), ("s2", [P, P], F32), ("dg", [P, N], F32)])
        k_rep = dg
        osq = dg
        go = vv
        late.close()
        early.close()

        bank = [ctx.enter_context(nc.psum_tensor(f"bank{i}", [P, 512], F32)) for i in range(8)]
        zb, (SA, SB, SC, TV, TK, OT) = bank[:2], bank[2:]

        ident = cst[:, C_ID:C_ID + P]

        def pcol(name, i):
            at = 0
            for n, r in PARAMS:
                if n == name:
                    return par[:, bass.ds(i + at, 1)]
                at += r

        raw_loaded = [sem("raw_loaded0"), sem("raw_loaded1")]
        hi_ready, lo_ready, piece_used, unit_read = (sem(n) for n in ("hi_ready", "lo_ready", "piece_used", "unit_read"))
        ident_loaded, masks_loaded, norm1_loaded, par_loaded, w0_loaded, wp_loaded, cache_loaded, s0_loaded = (
            sem(n) for n in ("ident_loaded", "masks_loaded", "norm1_loaded", "par_loaded", "w0_loaded", "wp_loaded",
                             "cache_loaded", "s0_loaded"))
        x_loaded = [[sem(f"x_loaded{half}{i}") for i in range(3)] for half in range(2)]
        fill_done, par_t, par_ready, lb_max, lb_exp, lb_ready = (
            sem(n) for n in ("fill_done", "par_t", "par_ready", "lb_max", "lb_exp", "lb_ready"))
        dve_link, newton_step = sem("dve_link"), sem("newton_step")
        ss_ready, rms_std, rms_diag, rms_bcast, rms_ready, stat_mm = (
            sem(n) for n in ("ss_ready", "rms_std", "rms_diag", "rms_bcast", "rms_ready", "stat_mm"))
        xt_t, xres_act, ahi_ready, alo_ready = (
            sem(n) for n in ("xt_t", "xres_act", "ahi_ready", "alo_ready"))
        t_ones, tails_ready, sc_zero, acc_zero, pad_zero, cache_tr, cache_in, win_step, win_ready, fix_ready, pooled_ready = (
            sem(n) for n in ("t_ones", "tails_ready", "sc_zero", "acc_zero", "pad_zero", "cache_tr", "cache_in", "win_step", "win_ready", "fix_ready",
                             "pooled_ready"))
        pool_mm, mp_hi_s, mp_lo_s, st_tr, st_copied, out_done = (
            sem(n) for n in ("pool_mm", "mp_hi_s", "mp_lo_s", "st_tr", "st_copied", "out_done"))
        zf_sig, f_ready, prod_ready, zq_sig, q_ready, qr_ready, kx_ready = (
            sem(n) for n in ("zf_sig", "f_ready", "prod_ready", "zq_sig", "q_ready",
                             "qr_ready", "kx_ready"))
        v_tr, k_tr, vt_ready, kt_ready, vm_ready, sc_mm, sc_put, put_go = (
            sem(n) for n in ("v_tr", "k_tr", "vt_ready", "kt_ready", "vm_ready", "sc_mm", "sc_put", "put_go"))
        v_thrice, k_thrice, v3_lo, k3_lo = (sem(n) for n in ("v_thrice", "k_thrice", "v3_lo", "k3_lo"))
        st_mm, s1_ready, s2_ready, s2_stored, sdec_ready, sn_mm, sn_ready, sn_stored = (
            sem(n) for n in ("st_mm", "s1_ready", "s2_ready", "s2_stored", "sdec_ready", "sn_mm", "sn_ready", "sn_stored"))
        o_mm, o_read, ostat_mm, ostd, orec, odiag, obc_mm, on_ready, mh_hi_s, mh_lo_s = (
            sem(n) for n in ("o_mm", "o_read", "ostat_mm", "ostd", "orec", "odiag", "obc_mm", "on_ready", "mh_hi_s",
                             "mh_lo_s"))
        g_sig, g_act, osum, gated, gm_hi, gm_lo = (
            sem(n) for n in ("g_sig", "g_act", "osum", "gated", "gm_hi", "gm_lo"))
        x1_sq, x1_acc, h2_hi, h2_lo = (sem(n) for n in ("x1_sq", "x1_acc", "h2_hi", "h2_lo"))
        gate_act, hid_ready, hid_hi, hid_lo = (
            sem(n) for n in ("gate_act", "hid_ready", "hid_hi", "hid_lo"))
        x2_scaled, x2_sq, x2_acc, last_sq, y_tr, y_copied, y_rec, y_scaled_a, y_scaled_v = (
            sem(n) for n in ("x2_scaled", "x2_sq", "x2_acc", "last_sq", "y_tr", "y_copied", "y_rec", "y_scaled_a",
                             "y_scaled_v"))

        block = ctx.enter_context(nc.Block())

        def after(eng, semaphore, value):
            if not isinstance(value, int) or value > 0:
                eng.wait_ge(semaphore, value)

        RMS_AT = 9
        AHEAD = 8
        def thrice(rep, src):
            return (rep[:, 0:6 * HS].rearrange("p (i c t) -> p i c t", i=2, c=3),
                    src[:, TP:N].rearrange("p (i t) -> p i t", i=2).unsqueeze(2).to_broadcast([P, 2, 3, HS]))

        HALF = ((0, 8), (8, 16))
        HALF_D = ((0, 8), (8, KB))

        Y_DVE = ((0, slice(0, 512)), (0, slice(512, 1024)), (1, slice(0, 1024)), (1, slice(1024, D)), (2, slice(0, D)))
        Y_ACT = ((0, slice(1024, D)),)

        def blocks_of(ap, level, n):
            return ap[:, 0:n].rearrange("p (m a j) -> p m a j", a=2, j=2 ** level)

        def times(level, n, lo):
            m = n // 2 ** (level + 1)
            return tl[level][:, 0:m, lo:lo + 2].unsqueeze(3).to_broadcast([P, m, 2, 2 ** level])

        def prod_in(level, which):
            m = (N if level < LS else TP) // 2 ** (level + 1)
            return tl[level][:, 0:m, which:which + 1].rearrange("p (m a) q -> p m (a q)", a=2)

        def right_half(ap, level):
            return ap.rearrange("p (m a j) -> p m a j", a=2, j=2 ** level)[:, :, 1, :]

        def load_params(eng, some, signal):
            at = 0
            for name, rows in PARAMS:
                if (name, rows) in some:
                    src = param_of[name]
                    src = src.rearrange("(r p) -> r p", p=P) if name == "norm_f" else src.rearrange("l (r p) -> (l r) p", p=P)
                    eng.dma_start(prow[at:at + rows, :], src).then_inc(signal, 16)
                at += rows

        def load_x(eng, half, i):
            cols = slice(half * HD, (half + 1) * HD)
            rows = P if i < 2 else NS
            src = x_prompt[0, i * P:(i + 1) * P, cols] if i < 2 else x_sample.rearrange("b t d -> (b t) d")[:, cols]
            eng.dma_start(xt[0:rows, i, cols], src).then_inc(x_loaded[half][i], 16)

        @block.sync
        def _(sp):
            def load(n, par_, view, tiles, col):
                after(sp, lo_ready, 2 * n - 2)
                k0, nk = tiles
                sp.dma_start(raw[:, par_, 0:nk * P].rearrange("p (k c) -> p k c", c=P),
                             view[:, bass.ds(k0, nk), bass.ds(col, P)]).then_inc(raw_loaded[par_], 16)

            sp.dma_start(cst[:, C_ID:C_ID + P], consts[:, C_ID:C_ID + P]).then_inc(ident_loaded, 16)
            load_x(sp, 0, 0)
            load_x(sp, 0, 2)
            w0 = raw[:, 0, :].rearrange("p (k c) -> p k c", c=P)
            k_mid = HALF[0][1]
            sp.dma_start(w0[:, 0:k_mid, :], win_v[:, 0:k_mid, 0:P]).then_inc(w0_loaded, 16)
            for i in range(3):
                load_x(sp, 1, i)
            sp.dma_start(w0[:, k_mid:KD, :], win_v[:, k_mid:KD, 0:P]).then_inc(raw_loaded[0], 16)
            load_params(sp, PARAMS[1:], par_loaded)
            load(1, 1, win_v, (0, KD), P)
            sp.dma_start(cache_t[:, :], cache_pool[0].rearrange("b t c -> (b t) c")).then_inc(cache_loaded, 16)
            load(2, 0, win_v, (0, KD), 2 * P)
            sp.dma_start(cst[:, C_MP:C_END], consts[:, C_MP:C_END]).then_inc(masks_loaded, 16)
            sp.dma_start(wp[:, :, :, :], w_pool[0].rearrange("g (k p) d -> p g k d", p=P)).then_inc(wp_loaded, 16)
            load(3, 1, win_v, (0, KD), 3 * P)
            with sp.Fori(2, (H0 // 2)) as i:
                for k in range(2):
                    load(2 * i + k, k, win_v, (0, KD), (2 * i + k) * P)
            with sp.Fori(0, HEADS // 2) as i:
                for k in range(2):
                    for j, part in enumerate((2, 1, 3)):
                        load(H0 + 6 * i + 3 * k + j, (3 * k + j) % 2, win_v, (0, KD),
                             part * PW + (2 * i + k) * P)
            with sp.Fori(0, HEADS // 2) as i:
                for k in range(2):
                    load(G0 + 2 * i + k, k, win_v, (0, KD), 4 * PW + (2 * i + k) * P)
            with sp.Fori(0, KD // 2) as i:
                for k in range(2):
                    load(O0 + 2 * i + k, k, wo_v, (0, KD), (2 * i + k) * P)
            with sp.Fori(0, BLOCKS) as b:
                with sp.Fori(0, KB) as j:
                    for k, view in enumerate((wg_v, wu_v)):
                        load(F0 + PER_BLOCK * b + 2 * j + k, k, view, (0, KD), (b * KB + j) * P)
                with sp.Fori(0, KD // 2) as j:
                    for k in range(2):
                        load(F0 + 2 * KB + PER_BLOCK * b + 2 * j + k, k, wd_v, (b * KB, KB), (2 * j + k) * P)
            for i, (t, cols) in enumerate(Y_DVE):
                dst = y_prompt[0, t * P:(t + 1) * P, cols] if t < 2 else y_sample.rearrange("b t d -> (b t) d")[:, cols]
                sp.wait_ge(y_scaled_v, i + 1)
                sp.dma_start(dst, yt[0:(P if t < 2 else NS), t, cols]).then_inc(out_done, 16)
            sp.wait_ge(s2_stored, 16 * HEADS)
            sp.wait_ge(sn_stored, 16 * HEADS)
            sp.wait_ge(out_done, 16 * (2 + len(Y_DVE) + len(Y_ACT)))

        @block.tensor
        def _(pe):
            def unit(n, par_, rhs, halves=HALF, between=(None, None), tile_wait=None,
                     after_tile=None):
                after(pe, unit_read, n - 1)
                last_k = halves[1][1] - 1
                for p, (k0, k1) in enumerate(halves):
                    pe.wait_ge(hi_ready, 2 * n + p + 1)
                    pe.wait_ge(lo_ready, 2 * n + p + 1)
                    for k in range(k0, k1):
                        if tile_wait is not None:
                            tile_wait(k)
                        r_hi, r_lo = rhs(k)
                        cols = slice(k * P, (k + 1) * P)
                        out = zb[par_][:, 0:N]
                        pe.matmul(out, whi[:, par_, cols], r_hi, start=(k == 0), stop=False)
                        pe.matmul(out, whi[:, par_, cols], r_lo, start=False, stop=False)
                        last = pe.matmul(out, wlo[:, par_, cols], r_hi, start=False, stop=(k == last_k))
                        if k == k1 - 1:
                            last.then_inc(piece_used, 1)
                        if after_tile is not None:
                            after_tile(k)
                    if between[p] is not None:
                        between[p]()

            def a_rhs(k):
                return a_hi[:, k, :], a_lo[:, k, :]

            def m_rhs(k):
                if k < HEADS:
                    return bp_hi[:, k, :], bp_lo[:, k, :]
                return bh_hi[:, k - HEADS, :], bh_lo[:, k - HEADS, :]

            def h_rhs(k):
                return h_hi[:, k, :], h_lo[:, k, :]

            def token_stats(out_bank, parts, which, signal):
                for i, (t0, t1) in enumerate(((0, P), (P, TP), (TP, N))):
                    for src in parts:
                        last = pe.matmul(out_bank[0:t1 - t0, i:i + 1], src[:, t0:t1], meanc[:, which:which + 1],
                                         start=src is parts[0], stop=src is parts[-1])
                last.then_inc(signal, 1)

            def to_all(out_bank, signal):
                pe.matmul(out_bank[:, 0:TP].rearrange("p (c t) -> p c t", c=2)[:, 0, :], ones[:, :], dg[:, 0:P],
                          start=True, stop=True)
                pe.matmul(out_bank[:, P:TP], ones[:, :], dg[:, P:TP], start=True, stop=True)
                pe.matmul(out_bank[:, TP:N], ones[0:NS, :], dg[0:NS, TP:N], start=True, stop=True).then_inc(signal, 1)

            def x_transposes(k):
                if k % (KD // 2) == 0:
                    for i in range(3):
                        pe.wait_ge(x_loaded[k // (KD // 2)][i], 16)
                b4 = (SA, SB, SC, TV)[k % 4]
                if k >= 4:
                    pe.wait_ge((xres_act, alo_ready)[k % 2], (k // 2 - 1, k - 3)[k % 2])
                pe.transpose(b4[:, 0:P], xt[:, 0, k * P:(k + 1) * P], ident)
                pe.transpose(b4[:, P:TP], xt[:, 1, k * P:(k + 1) * P], ident)
                pe.transpose(b4[:, TP:N], xt[0:NS, 2, k * P:(k + 1) * P], ident[0:NS, 0:NS]).then_inc(xt_t, 1)

            pe.wait_ge(ident_loaded, 16)
            pe.wait_ge(norm1_loaded, 16)
            pe.transpose(TK[:, 0:KD], prow[0:KD, :], ident[0:KD, 0:KD]).then_inc(par_t, 1)
            for k in range(AHEAD):
                x_transposes(k)

            def x_tile(k):
                if k + AHEAD < KD:
                    x_transposes(k + AHEAD)
                if k == 2:
                    pe.wait_ge(par_loaded, 16 * (len(PARAMS) - 1))
                    pe.transpose(TK[:, P:P + n_par], prow, ident[0:n_par, 0:n_par]).then_inc(par_t, 1)
                pe.wait_ge(ahi_ready, k + 1)
                pe.wait_ge(alo_ready, k + 1)

            def rms_first():
                pe.wait_ge(fill_done, 3)
                pe.wait_ge(rms_diag, 1)
                to_all(TK, rms_bcast)

            def cache_tiles(g):
                pe.wait_ge(cache_loaded, 16)
                after(pe, cache_in, g)
                for c in range(2):
                    cols = slice((2 * g + c) * P, (2 * g + c + 1) * P)
                    last = pe.transpose(OT[:, c * P:c * P + NB * CACHE], cache_t[:, cols],
                                        ident[0:NB * CACHE, 0:NB * CACHE])
                last.then_inc(cache_tr, 1)

            def pool_states(g):
                pe.wait_ge(tails_ready, g + 1)
                after(pe, st_copied, g)
                for c in range(2):
                    pe.transpose(TK[0:NB * CACHE, c * P:(c + 1) * P], tails[:, c, 0:NB * CACHE], ident)
                    last = pe.transpose(TK[0:CACHE, TP + c * P:TP + (c + 1) * P], tails[:, c, NB * CACHE:], ident)
                last.then_inc(st_tr, 1)

            def pool_product(g):
                pe.wait_ge(wp_loaded, 16)
                pe.wait_ge(pooled_ready, g + 1)
                for ct, bk in enumerate((SA, SB)):
                    if g >= 1:
                        pe.wait_ge(mp_lo_s, 2 * (g - 1) + ct + 1)
                    for kc in range(2):
                        last = pe.matmul(bk[:, 0:N], wp[:, g, kc, ct * P:(ct + 1) * P], pooled[:, kc, :],
                                         start=(kc == 0), stop=(kc == 1))
                    last.then_inc(pool_mm, 1)

            for g in range(NG):
                def first(g=g):
                    cache_tiles(g)
                    if g >= 1:
                        pool_states(g - 1)

                def third(g=g):
                    if g >= 1:
                        pool_product(g - 1)
                if g == 0:
                    unit(U0, 0, a_rhs, between=(None, first), tile_wait=x_tile)
                else:
                    unit(U0 + 2 * g, 0, a_rhs, between=(first, None))

                def spread_rms(k):
                    if k == RMS_AT:
                        rms_first()
                unit(U0 + 2 * g + 1, 1, a_rhs, between=(None, third), after_tile=spread_rms if g == 0 else None)

            def sample_thrice(bk, rep):
                for i in range(2):
                    last = pe.transpose(bk[0:3 * HS, TP + i * P:TP + (i + 1) * P], rep[:, i * 3 * HS:(i + 1) * 3 * HS],
                                        ident)
                return last

            def rec_scores(r):
                pe.wait_ge(kx_ready, (LP + 1) * (r + 1))
                pe.wait_ge(k_thrice, r + 1)
                after(pe, k3_lo, r)
                pe.transpose(TK[:, 0:P], kx[LP][:, 0:P], ident)
                pe.transpose(TK[:, P:TP], kx[LP][:, P:TP], ident)
                sample_thrice(TK, k_rep).then_inc(k_tr, 1)
                pe.wait_ge(unit_read, H0 + 3 * r + 3)
                pe.wait_ge(v_thrice, r + 1)
                after(pe, ostd, r)
                pe.transpose(TV[:, 0:P], vv[:, 0:P], ident)
                pe.transpose(TV[:, P:TP], vv[:, P:TP], ident)
                sample_thrice(TV, v_rep).then_inc(v_tr, 1)
                pe.wait_ge(q_ready, r + 1)
                pe.wait_ge(qr_ready, (LP + 1) * (r + 1))
                after(pe, s2_ready, r)
                after(pe, sn_ready, r)

                def level(bk, at, l):
                    for c in range(NC):
                        last = pe.matmul(bk[:, at + c * 64:at + c * 64 + 64].rearrange("p (m j) -> p m j", j=2 ** l),
                                         kx[l][:, c * CH:(c + 1) * CH], right_half(qr[l][:, c * CH:(c + 1) * CH], l),
                                         start=True, stop=True)
                    return last
                for l in range(4, LP):
                    last = level(SC, (l - 4) * P, l)
                last.then_inc(sc_mm, 1)
                for c in range(NC):
                    pe.matmul(SA[:, c * CH:(c + 1) * CH], kx[0][:, c * CH:(c + 1) * CH], qq[:, c * CH:(c + 1) * CH],
                              start=True, stop=True)
                last = pe.matmul(SA[0:NS, TP:N], kx[0][:, TP:N], qq[:, TP:N], start=True, stop=True)
                for l in range(LS):
                    last = pe.matmul(SA[0:NS, N + 32 * l:N + 32 * l + 32].rearrange("p (m j) -> p m j", j=2 ** l),
                                     kx[l][:, TP:N], right_half(qr[l][:, TP:N], l), start=True, stop=True)
                last.then_inc(sc_mm, 1)
                for l in range(4):
                    last = level(SB, l * P, l)
                last.then_inc(sc_mm, 1)

            def rec_s0(r, b):
                if b == 0:
                    pe.wait_ge(s0_loaded, 16 * (r + 1))
                    after(pe, on_ready, r)
                t = slice(TP + b * TS, TP + (b + 1) * TS)
                pe.matmul(OT[:, t], s0[:, b, :], qr[LS][:, t], start=(b == 0), stop=False)

            def rec_state(r):
                pe.wait_ge(vt_ready, r + 1)
                pe.wait_ge(kt_ready, r + 1)
                pe.wait_ge(sc_put, PUTS * r + LP - 4)
                for c in range(NC):
                    last = pe.matmul(SC[:, c * P:(c + 1) * P], kt[:, c, :], vt[:, c, :], start=True, stop=True)
                last.then_inc(st_mm, 1)

            def rec_out(r):
                pe.wait_ge(s1_ready, r + 1)
                pe.wait_ge(sc_put, PUTS * (r + 1))
                pe.matmul(OT[:, 0:CH], vt[:, 0, :], sc[:, 0, :], start=False, stop=False)
                pe.matmul(OT[:, CH:TP], vt[:, 1, :], sc[:, 1, :], start=False, stop=False)
                pe.matmul(OT[:, CH:TP], s1[:, :], qr[LP][:, CH:TP], start=False, stop=False)
                pe.matmul(OT[:, TP:N], vt[0:NS, 2, :], scs[:, :], start=False, stop=True).then_inc(o_mm, 1)
                pe.wait_ge(vm_ready, r + 1)
                pe.wait_ge(k3_lo, r + 1)
                for i, bk in enumerate((SA, SB)):
                    last = pe.matmul(bk[:, :].rearrange("p (b v) -> p b v", v=P), k3[:, i, :], vm[:, i, :, :],
                                     start=True, stop=True)
                last.then_inc(sn_mm, 1)

            def rec_stat(r):
                pe.wait_ge(o_read, 2 * (r + 1))
                token_stats(TV, (osq,), 1, ostat_mm)

            def rec_bcast(r):
                pe.wait_ge(odiag, r + 1)
                to_all(OT, obc_mm)

            def window(n, par_, r, extra=(None, None), last=False):
                def at(f):
                    return (lambda: f(r)) if r is not None else None
                unit(n, par_, a_rhs, between=(at(rec_scores) if r is not None else extra[0], at(rec_state)))
                def s0_part(k):
                    if k < NB:
                        rec_s0(r, k)
                unit(n + 1, 1 - par_, a_rhs, between=(at(rec_out), at(rec_stat)),
                     after_tile=s0_part if r is not None else None)
                unit(n + 2, par_, a_rhs, between=(extra[1], at(rec_bcast) if not last else None))

            window(H0, 0, None, (lambda: pool_states(NG - 1), lambda: pool_product(NG - 1)))
            window(H0 + 3, 1, 0)
            with pe.Fori(0, (HEADS - 2) // 2) as i:
                window(H0 + 6 + 6 * i, 0, 2 * i + 1)
                window(H0 + 9 + 6 * i, 1, 2 * i + 2)
            window(G0, 0, HEADS - 1, last=True)

            def last_bcast(k):
                if k == 4:
                    rec_bcast(HEADS - 1)
            unit(G0 + 3, 1, a_rhs, after_tile=last_bcast)
            with pe.Fori(0, (HEADS - 4) // 2) as i:
                for k in range(2):
                    unit(G0 + 4 + 2 * i + k, k, a_rhs)

            def m_tile(k):
                if k == 0:
                    pe.wait_ge(mp_lo_s, HEADS)
                if k >= HEADS:
                    pe.wait_ge(gm_hi, k - HEADS + 1)
                    pe.wait_ge(gm_lo, k - HEADS + 1)
            unit(O0, 0, m_rhs, tile_wait=m_tile)
            unit(O0 + 1, 1, m_rhs)
            with pe.Fori(1, KD // 2) as i:
                for k in range(2):
                    unit(O0 + 2 * i + k, k, m_rhs)

            def a2_tile(k):
                pe.wait_ge(h2_hi, k + 1)
                pe.wait_ge(h2_lo, k + 1)

            def rms_second():
                pe.wait_ge(x1_acc, KD)
                token_stats(TV, (acc,), 0, stat_mm)

            def rms_second_all():
                pe.wait_ge(rms_diag, 2)
                to_all(TK, rms_bcast)

            def ffn(b, first, final):
                n0 = F0 + PER_BLOCK * b
                if first:
                    def spread_second(k):
                        if k == 1:
                            rms_second_all()
                    unit(n0, 0, a_rhs, between=(rms_second, None), tile_wait=a2_tile)
                    unit(n0 + 1, 1, a_rhs, after_tile=spread_second)
                with pe.Fori(1 if first else 0, KB) as j:
                    unit(n0 + 2 * j, 0, a_rhs)
                    unit(n0 + 2 * j + 1, 1, a_rhs)
                nd = n0 + 2 * KB

                def h_tile(k):
                    pe.wait_ge(hid_hi, KB * b + k + 1)
                    pe.wait_ge(hid_lo, KB * b + k + 1)

                def y_tiles(j, par_):
                    def go():
                        pe.wait_ge(x2_scaled, j + 1)
                        after(pe, y_copied, j - 1)
                        bk = (SA, SB)[par_]
                        for i, (t0, t1) in enumerate(((0, P), (P, TP), (TP, N))):
                            last = pe.transpose(bk[0:t1 - t0, i * P:(i + 1) * P], x2g[:, par_, t0:t1], ident)
                        last.then_inc(y_tr, 1)
                    return go

                unit(nd, 0, h_rhs, HALF_D, tile_wait=h_tile)
                unit(nd + 1, 1, h_rhs, HALF_D, between=(None, y_tiles(0, 0) if final else None))
                if final:
                    for k in range(2):
                        unit(nd + 2 + k, k, h_rhs, HALF_D, between=(None, y_tiles(1 + k, 1 - k)))
                with pe.Fori(2 if final else 1, KD // 2) as j:
                    for k in range(2):
                        unit(nd + 2 * j + k, k, h_rhs, HALF_D,
                             between=(None, y_tiles(2 * j + k - 1, 1 - k) if final else None))
                if final:
                    pe.wait_ge(x2_acc, KD - 1)
                    pe.wait_ge(last_sq, 1)
                    token_stats(TV, (acc, sq), 0, stat_mm)
                    y_tiles(KD - 1, 1)()

            ffn(0, True, False)
            with pe.Fori(1, BLOCKS - 1) as b:
                ffn(b, False, False)
            ffn(BLOCKS - 1, False, True)

        @block.scalar
        def _(act):
            def split_hi(n, par_, halves=HALF):
                act.wait_ge(raw_loaded[par_], 8 * (n - par_) + 16)
                for p, tiles in enumerate(halves):
                    hi_piece(n, par_, p, tiles)

            def hi_piece(n, par_, p, tiles):
                k0, k1 = tiles
                after(act, piece_used, 2 * n + p - 3)
                act.activation(whi[:, par_, k0 * P:k1 * P], raw[:, par_, k0 * P:k1 * P], ACT.Copy)\
                   .then_inc(hi_ready, 1)

            load_params(act, PARAMS[:1], norm1_loaded)
            load_x(act, 0, 1)
            act.wait_ge(fill_done, 3)
            act.activation(warm[:, 0:1], epst[:, 0:1], ACT.Sqrt)

            def square(half, i):
                rows, at = (P if i < 2 else NS), 2 * i + half
                act.wait_ge(x_loaded[half][i], 16)
                after(act, ss_ready, 3 * half + i)
                act.activation(junk[0:rows, :], xt[0:rows, i, half * HD:(half + 1) * HD], ACT.Square,
                               accum_out=stat[0:rows, at:at + 1]).then_inc(ss_ready, 1)

            for i in range(2):
                square(0, i)
            act.wait_ge(par_ready, 1)
            for k in range(KD):
                act.wait_ge(xt_t, k + 1)
                bk = (SA, SB, SC, TV)[k % 4]
                act.activation(a_hi[:, k, :], bk[:, 0:N], ACT.Copy, scale=pcol("norm1", k)).then_inc(ahi_ready, 1)
                if k % 2 == 0:
                    act.activation(x1[:, k, :], bk[:, 0:N], ACT.Copy).then_inc(xres_act, 1)
                if k == 1:
                    act.wait_ge(w0_loaded, 16)
                    hi_piece(0, 0, 0, HALF[0])
                if k == 3:
                    square(0, 2)
                if k == 8:
                    act.wait_ge(raw_loaded[0], 16)
                    hi_piece(0, 0, 1, HALF[1])
            split_hi(1, 1)
            for i in range(3):
                square(1, i)
            act.wait_ge(ss_ready, 7)
            act.activation(stat[:, 9:12], stat[:, 6:9], ACT.Sqrt, bias=epst[:, 0:1], scale=1.0 / D).then_inc(rms_std, 1)
            act.wait_ge(lb_max, 1)
            act.activation(lbt[:, 1:3, :], lbt[:, 1:3, :], ACT.Exp).then_inc(lb_exp, 1)

            def cache_copy(g):
                act.wait_ge(cache_tr, g + 1)
                after(act, pooled_ready, g - 1)
                act.wait_ge(pad_zero, 1)
                for c in range(2):
                    seqs = uu[:, g % 2, c, CACHE + TP:UW].rearrange("p (b t) -> p b t", b=NB)[:, :, 0:CACHE]
                    last = act.activation(seqs, OT[:, c * P:c * P + NB * CACHE].rearrange("p (b t) -> p b t", b=NB),
                                          ACT.Copy)
                last.then_inc(cache_in, 1)

            def tail_copy(g):
                act.wait_ge(unit_read, U0 + 2 * g + 2)
                after(act, st_tr, g)
                for c in range(2):
                    row = uu[:, g % 2, c, :]
                    act.activation(tails[:, c, 0:NB * CACHE].rearrange("p (b t) -> p b t", b=NB),
                                   row[:, CACHE + TP:UW].rearrange("p (b t) -> p b t", b=NB)[:, :, TS:TS + CACHE],
                                   ACT.Copy)
                    last = act.activation(tails[:, c, NB * CACHE:], row[:, TP:TP + CACHE], ACT.Copy)
                last.then_inc(tails_ready, 1)

            def state_copy(g):
                act.wait_ge(st_tr, g + 1)
                act.activation(st_s[:, g * TP:(g + 1) * TP], TK[0:NB * CACHE, 0:TP], ACT.Copy)
                act.activation(st_p[:, g * TP:(g + 1) * TP], TK[0:CACHE, TP:2 * TP], ACT.Copy).then_inc(st_copied, 1)

            def pool_hi(g):
                for ct, bk in enumerate((SA, SB)):
                    j = 2 * g + ct
                    act.wait_ge(pool_mm, j + 1)
                    act.activation(bp_hi[:, j, :], bk[:, 0:N], ACT.Copy, scale=pcol("pool_scale", j)).then_inc(mp_hi_s, 1)

            for g in range(NG):
                if g >= 1:
                    split_hi(U0 + 2 * g + 1, 1)
                    tail_copy(g - 1)
                cache_copy(g)
                if g >= 1:
                    state_copy(g - 1)
                split_hi(U0 + 2 * g + 2, 0)
                if g >= 1:
                    pool_hi(g - 1)

            def forget(h):
                act.wait_ge(unit_read, H0 + 3 * h + 1)
                after(act, q_ready, h)
                act.activation(sgm[:, :], zf[:, :], ACT.Sigmoid).then_inc(zf_sig, 1)
                after(act, kx_ready, (LP + 1) * h)
                after(act, qr_ready, (LP + 1) * h)
                act.wait_ge(zf_sig, h + 1)
                act.activation(tl[0][:, :, 1:3], sgm[:, :].rearrange("p (m a) -> p m a", a=2), ACT.Identity,
                               bias=lbt[:, 4, bass.ds(h, 1)], scale=lbt[:, 5, bass.ds(h, 1)]).then_inc(f_ready, 1)

            def sigmoid_q(h):
                act.wait_ge(unit_read, H0 + 3 * h + 2)
                act.wait_ge(f_ready, h + 1)
                act.activation(sgm[:, :], zq[:, :], ACT.Sigmoid).then_inc(zq_sig, 1)

            def rec_tokens(r):
                act.wait_ge(k_tr, r + 1)
                after(act, sn_mm, r)
                act.activation(kt[:, 0:2, :], TK[:, 0:TP].rearrange("p (c v) -> p c v", c=2), ACT.Copy)
                act.activation(k3[:, :, :], TK[0:3 * HS, TP:TP + 2 * P].rearrange("p (i v) -> p i v", i=2), ACT.Copy)\
                   .then_inc(kt_ready, 1)
                act.wait_ge(v_tr, r + 1)
                act.activation(vt[:, 0:2, :], TV[:, 0:TP].rearrange("p (c v) -> p c v", c=2), ACT.Copy)
                for i in range(2):
                    rows = slice(i * HS, (i + 1) * HS)
                    act.activation(vt[rows, 2, :], TV[rows, TP + i * P:TP + (i + 1) * P], ACT.Copy)
                act.activation(v3[:, :, :], TV[0:3 * HS, TP:TP + 2 * P].rearrange("p (i v) -> p i v", i=2), ACT.Copy)\
                   .then_inc(vt_ready, 1)

            def rec_squares(r):
                act.wait_ge(o_mm, r + 1)
                after(act, on_ready, r)
                act.activation(osq[:, :], OT[:, 0:N], ACT.Square).then_inc(o_read, 1)
                act.activation(osb[:, :], OT[:, 0:N], ACT.Copy).then_inc(o_read, 1)

            def load_s0(h):
                act.wait_ge(o_mm, h)
                act.wait_ge(sdec_ready, h)
                act.dma_start(s0[:, :, :], state_hgrn[0, :, bass.ds(h, 1), :, :].rearrange("b o k v -> k (b o) v"))\
                   .then_inc(s0_loaded, 16)

            def rec_stores(r):
                act.wait_ge(s2_ready, r + 1)
                act.dma_start(hgrn_prompt[0, 0, bass.ds(r, 1), :, :].rearrange("o k v -> k (o v)"), s2[:, :])\
                   .then_inc(s2_stored, 16)
                act.wait_ge(sn_ready, r + 1)
                act.dma_start(hgrn_sample[0, :, bass.ds(r, 1), :, :].rearrange("b o k v -> k (b o) v"), sn[:, :, :])\
                   .then_inc(sn_stored, 16)

            def rec_std(r):
                act.wait_ge(ostat_mm, r + 1)
                after(act, odiag, r)
                act.activation(stat[:, 6:8], TV[:, 0:2], ACT.Identity, bias=epst[:, 0:1])
                act.activation(stat[0:NS, 8:9], TV[0:NS, 2:3], ACT.Identity, bias=epst[0:NS, 0:1])
                act.activation(stat[:, 0:2], TV[:, 0:2], ACT.Sqrt, bias=epst[:, 0:1])
                act.activation(stat[0:NS, 2:3], TV[0:NS, 2:3], ACT.Sqrt, bias=epst[0:NS, 0:1]).then_inc(ostd, 1)

            def rec_hi(r):
                act.wait_ge(on_ready, r + 1)
                act.activation(bh_hi[:, r, :], on[:, :], ACT.Copy).then_inc(mh_hi_s, 1)

            def gate(h):
                gate_sigmoid(h)
                gate_split(h)

            def gate_sigmoid(h):
                act.wait_ge(unit_read, G0 + h + 1)
                act.activation(sgm[:, :], zf[:, :], ACT.Sigmoid).then_inc(g_sig, 1)

            def gate_split(h):
                act.wait_ge(gated, h + 1)
                act.activation(bh_hi[:, h, :], go[:, :], ACT.Copy).then_inc(gm_hi, 1)

            def window(n, par_, h, r):
                split_hi(n + 1, 1 - par_)
                rec_tokens(r)
                forget(h) if h is not None else gate(0)
                split_hi(n + 2, par_)
                rec_squares(r)
                if h is not None:
                    load_s0(r + 1)
                rec_stores(r)
                sigmoid_q(h) if h is not None else gate(1)
                split_hi(n + 3, 1 - par_)
                rec_std(r)
                if h is None:
                    gate(2)
                else:
                    rec_hi(r)

            split_hi(H0 + 1, 1)
            tail_copy(NG - 1)
            state_copy(NG - 1)
            act.wait_ge(st_copied, NG)
            act.dma_start(pool_sample[0].rearrange("b t c -> (b t) c"), st_s[:, :]).then_inc(out_done, 16)
            act.dma_start(pool_prompt[0, 0], st_p[:, :]).then_inc(out_done, 16)
            act.wait_ge(t_ones, 1)
            forget(0)
            split_hi(H0 + 2, 0)
            sigmoid_q(0)
            split_hi(H0 + 3, 1)
            pool_hi(NG - 1)
            act.wait_ge(sc_zero, 1)
            act.dma_start(s0[:, :, :], state_hgrn[0, :, 0, :, :].rearrange("b k v -> k b v")).then_inc(s0_loaded, 16)
            window(H0 + 3, 1, 1, 0)
            with act.Fori(0, (HEADS - 2) // 2) as i:
                window(H0 + 6 + 6 * i, 0, 2 * i + 2, 2 * i + 1)
                window(H0 + 9 + 6 * i, 1, 2 * i + 3, 2 * i + 2)
            act.wait_ge(out_done, 32)
            window(G0, 0, None, HEADS - 1)
            split_hi(G0 + 4, 0)
            gate_sigmoid(3)
            rec_hi(HEADS - 1)
            gate_split(3)
            with act.Fori(0, (HEADS - 4) // 2) as i:
                for k in range(2):
                    split_hi(G0 + 5 + 2 * i + k, 1 - k)
                    gate(4 + 2 * i + k)

            def h2_part(j):
                act.wait_ge(unit_read, O0 + j + 1)
                act.activation(a_hi[:, j, :], x1[:, j, :], ACT.Copy, scale=pcol("norm2", j)).then_inc(h2_hi, 1)

            with act.Fori(0, KD // 2) as i:
                for k in range(2):
                    split_hi(O0 + 1 + 2 * i + k, 1 - k)
                    h2_part(2 * i + k)

            def silu(n):
                act.wait_ge(unit_read, n + 1)
                act.activation(sg[:, :], zg[:, :], ACT.Silu).then_inc(gate_act, 1)

            def hidden_hi(c, j):
                act.wait_ge(hid_ready, c + 1)
                act.activation(h_hi[:, j, :], hid[:, :], ACT.Copy).then_inc(hid_hi, 1)

            def ffn(b, first, final):
                n0 = F0 + PER_BLOCK * b

                def pair(j, halves):
                    split_hi(n0 + 2 * j + 1, 1)
                    silu(n0 + 2 * j)
                    split_hi(n0 + 2 * j + 2, 0, halves)
                    hidden_hi(KB * b + j, j)
                if first:
                    split_hi(n0 + 1, 1)
                    act.wait_ge(stat_mm, 1)
                    act.activation(stat[:, 6:8], TV[:, 0:2], ACT.Identity, bias=epst[:, 0:1])
                    act.activation(stat[0:NS, 8:9], TV[0:NS, 2:3], ACT.Identity, bias=epst[0:NS, 0:1])
                    act.activation(stat[:, 0:2], TV[:, 0:2], ACT.Sqrt, bias=epst[:, 0:1])
                    act.activation(stat[0:NS, 2:3], TV[0:NS, 2:3], ACT.Sqrt, bias=epst[0:NS, 0:1]).then_inc(rms_std, 1)
                    silu(n0)
                    split_hi(n0 + 2, 0)
                    hidden_hi(0, 0)
                with act.Fori(1 if first else 0, KB - 1) as j:
                    pair(j, HALF)
                pair(KB - 1, HALF_D)
                nd = n0 + 2 * KB

                def y_part(j, par_):
                    act.wait_ge(unit_read, nd + j + 1)
                    after(act, y_tr, j - 1)
                    act.activation(x2g[:, par_, :], x2[:, par_, :], ACT.Copy, scale=pcol("norm_f", j))\
                       .then_inc(x2_scaled, 1)

                def y_copy(j, par_):
                    act.wait_ge(y_tr, j + 1)
                    bk = (SA, SB)[par_]
                    act.activation(yt[:, 0:2, bass.ds(j * P, P)], bk[:, 0:TP].rearrange("p (c v) -> p c v", c=2),
                                   ACT.Copy)
                    act.activation(yt[0:NS, 2, bass.ds(j * P, P)], bk[0:NS, TP:TP + P], ACT.Copy).then_inc(y_copied, 1)

                if not final:
                    with act.Fori(0, KD // 2 - 1) as j:
                        split_hi(nd + 2 * j + 1, 1, HALF_D)
                        split_hi(nd + 2 * j + 2, 0, HALF_D)
                    split_hi(nd + KD - 1, 1, HALF_D)
                    split_hi(nd + KD, 0)
                else:
                    split_hi(nd + 1, 1, HALF_D)
                    y_part(0, 0)
                    split_hi(nd + 2, 0, HALF_D)
                    act.activation(warm[:, 1:2], epst[:, 0:1], ACT.Sqrt)
                    y_part(1, 1)
                    y_copy(0, 0)
                    with act.Fori(1, KD // 2 - 1) as j:
                        split_hi(nd + 2 * j + 1, 1, HALF_D)
                        y_part(2 * j, 0)
                        y_copy(2 * j - 1, 1)
                        split_hi(nd + 2 * j + 2, 0, HALF_D)
                        y_part(2 * j + 1, 1)
                        y_copy(2 * j, 0)
                    split_hi(nd + KD - 1, 1, HALF_D)
                    y_part(KD - 2, 0)
                    y_copy(KD - 3, 1)
                    y_part(KD - 1, 1)
                    y_copy(KD - 2, 0)
                    act.wait_ge(stat_mm, 2)
                    act.activation(stat[:, 0:2], TV[:, 0:2], ACT.Sqrt, bias=epst[:, 0:1])
                    act.activation(stat[0:NS, 2:3], TV[0:NS, 2:3], ACT.Sqrt, bias=epst[0:NS, 0:1])
                    act.activation(stat[:, 6:8], TV[:, 0:2], ACT.Identity, bias=epst[:, 0:1])
                    act.activation(stat[0:NS, 8:9], TV[0:NS, 2:3], ACT.Identity, bias=epst[0:NS, 0:1])\
                       .then_inc(rms_std, 1)
                    y_copy(KD - 1, 1)

            ffn(0, True, False)
            with act.Fori(1, BLOCKS - 1) as b:
                ffn(b, False, False)
            ffn(BLOCKS - 1, False, True)
            act.wait_ge(y_rec, 2)
            act.wait_ge(y_copied, KD)
            for i, (t, cols) in enumerate(Y_ACT):
                act.activation(yt[:, t, cols], yt[:, t, cols], ACT.Copy, scale=stat[:, 9 + t:10 + t]).then_inc(y_scaled_a, 1)
                act.wait_ge(y_scaled_a, i + 1)
                act.dma_start(y_prompt[0, t * P:(t + 1) * P, cols], yt[:, t, cols]).then_inc(out_done, 16)

        @block.vector
        def _(dve):
            links = [0]

            def link(ins):
                links[0] += 1
                ins.then_inc(dve_link, 1)
                dve.wait_ge(dve_link, links[0])

            def split_lo(n, par_, halves=HALF):
                for p, tiles in enumerate(halves):
                    lo_piece(n, par_, p, tiles)

            def lo_piece(n, par_, p, tiles):
                dve.wait_ge(hi_ready, 2 * n + p + 1)
                cols = slice(tiles[0] * P, tiles[1] * P)
                dve.tensor_tensor(wlo[:, par_, cols], raw[:, par_, cols], whi[:, par_, cols].bitcast(F32), SUB)\
                   .then_inc(lo_ready, 1)

            def done(n):
                dve.wait_ge(piece_used, 2 * n + 2)

            def scaled(n, par_, out):
                done(n)
                return dve.tensor_tensor(out, zb[par_][:, 0:N], rbc[:, :], MUL)

            def split_rest(out_lo, src, out_hi):
                return dve.tensor_tensor(out_lo, src, out_hi.bitcast(F32), SUB)

            dve.memset(ones[:, :], 1.0).then_inc(fill_done, 1)
            dve.memset(meanc[:, 0:1], 1.0 / D)
            dve.memset(meanc[:, 1:2], 1.0 / P)
            dve.memset(epst[:, :], EPS).then_inc(fill_done, 1)
            dve.memset(stat[:, :], 0.5).then_inc(fill_done, 1)
            dve.wait_ge(par_t, 1)
            dve.tensor_copy(par[:, 0:KD], TK[:, 0:KD]).then_inc(par_ready, 1)
            dve.wait_ge(par_ready, 1)

            def lower_bound_max():
                dve.wait_ge(par_t, 2)
                dve.tensor_copy(par[:, KD:n_par], TK[:, P + KD:P + n_par]).then_inc(par_ready, 1)
                dve.wait_ge(par_ready, 2)
                lb0 = 3 * KD
                rows = par[:, lb0:lb0 + 2 * HEADS].rearrange("p (r h) -> p r h", r=2)
                link(dve.tensor_tensor(lbt[:, 0, :], rows[:, 0, :], rows[:, 1, :], ALU.max))
                dve.tensor_tensor(lbt[:, 1, :], rows[:, 0, :], lbt[:, 0, :], SUB)
                dve.tensor_tensor(lbt[:, 2, :], rows[:, 1, :], lbt[:, 0, :], SUB).then_inc(lb_max, 1)

            def lower_bound():
                dve.wait_ge(lb_exp, 1)
                link(dve.tensor_tensor(lbt[:, 3, :], lbt[:, 1, :], lbt[:, 2, :], ADD))
                link(dve.reciprocal(lbt[:, 0, :], lbt[:, 3, :]))
                link(dve.tensor_tensor(lbt[:, 4, :], lbt[:, 1, :], lbt[:, 0, :], MUL))
                dve.tensor_scalar(lbt[:, 5, :], lbt[:, 4, :], -1.0, 1.0, MUL, ADD).then_inc(lb_ready, 1)

            for k in range(KD):
                bk = (SA, SB, SC, TV)[k % 4]
                dve.wait_ge(ahi_ready, k + 1)
                if k % 2 == 1:
                    dve.tensor_copy(x1[:, k, :], bk[:, 0:N])
                else:
                    dve.wait_ge(xres_act, k // 2 + 1)
                src = (x1[:, k, :], bk[:, 0:N])[k % 2]
                dve.scalar_tensor_tensor(out=a_lo[:, k, :], in0=src, scalar=pcol("norm1", k),
                                         in1=a_hi[:, k, :].bitcast(F32), op0=MUL, op1=SUB).then_inc(alo_ready, 1)
                if k == 3:
                    lo_piece(0, 0, 0, HALF[0])
                if k == 9:
                    lo_piece(0, 0, 1, HALF[1])
                if k == 12:
                    lower_bound_max()
            split_lo(1, 1)
            dve.wait_ge(ss_ready, 6)
            ss = stat[:, 0:6].rearrange("p (i h) -> p i h", h=2)
            dve.tensor_tensor(stat[:, 6:9], ss[:, :, 0], ss[:, :, 1], ADD).then_inc(ss_ready, 1)

            def newton(y, mean, tmp):
                def step(ins):
                    newtons[0] = newtons[0] + 1
                    ins.then_inc(newton_step, 1)
                    dve.wait_ge(newton_step, newtons[0])
                step(dve.tensor_tensor(tmp, y, y, MUL))
                step(dve.tensor_tensor(tmp, tmp, mean, MUL))
                step(dve.tensor_scalar(tmp, tmp, -0.5, 1.5, MUL, ADD))
                step(dve.tensor_tensor(y, y, tmp, MUL))

            def diagonals(src, signal):
                dve.tensor_tensor(dg[:, 0:TP].rearrange("p (c t) -> p c t", c=2),
                                  ident.unsqueeze(1).to_broadcast([P, 2, P]),
                                  stat[:, src:src + 2].unsqueeze(2).to_broadcast([P, 2, P]), MUL)
                dve.tensor_scalar(dg[0:NS, TP:N], ident[0:NS, 0:NS], stat[0:NS, src + 2:src + 3], None, MUL)\
                   .then_inc(signal, 1)

            def rms_row(count):
                dve.wait_ge(rms_bcast, count)
                dve.tensor_copy(rbc[:, :], TK[:, 0:N]).then_inc(rms_ready, 1)
                dve.wait_ge(rms_ready, count)

            dve.wait_ge(rms_std, 1)
            link(dve.tensor_scalar(stat[:, 3:6], stat[:, 6:9], 1.0 / D, EPS, MUL, ADD))
            link(dve.reciprocal(stat[:, 6:9], stat[:, 9:12]))
            newtons = [0]
            newton(stat[:, 6:9], stat[:, 3:6], stat[:, 0:3])
            diagonals(6, rms_diag)
            lower_bound()

            dve.wait_ge(pad_zero, 1)
            dve.wait_ge(masks_loaded, 16)

            def u_part(ft):
                g, c = ft // 2, ft % 2
                done(U0 + ft)
                after(dve, pooled_ready, g - 1)
                after(dve, tails_ready, g - 1)
                row = uu[:, g % 2, c, :]
                dve.tensor_tensor(row[:, CACHE:CACHE + TP], zb[c][:, 0:TP], rbc[:, 0:TP], MUL)
                dve.tensor_tensor(row[:, CACHE + TP:UW].rearrange("p (b t) -> p b t", b=NB)[:, :, CACHE:CACHE + TS],
                                  zb[c][:, TP:N].rearrange("p (b t) -> p b t", b=NB),
                                  rbc[:, TP:N].rearrange("p (b t) -> p b t", b=NB), MUL).then_inc(unit_read, 1)

            def pool_means(g):
                win = (wa, wb, wa, wb)[g]
                inv = 1.0 / WINDOWS[g]
                dve.wait_ge(win_ready, g + 1)
                after(dve, pool_mm, 2 * g)
                dve.tensor_tensor(pooled[:, :, 0:16], win[:, :, CACHE:CACHE + 16],
                                  cst[:, C_IC + 16 * g:C_IC + 16 * g + 16].unsqueeze(1).to_broadcast([P, 2, 16]),
                                  MUL).then_inc(fix_ready, 1)
                for c in range(2):
                    def seqs(ap):
                        return ap[:, c, CACHE + TP:UW].rearrange("p (b t) -> p b t", b=NB)[:, :, CACHE:CACHE + TS]
                    dve.scalar_tensor_tensor(out=pooled[:, c, TP:N].rearrange("p (b t) -> p b t", b=NB),
                                             in0=seqs(win), scalar=inv, in1=seqs(uu[:, g % 2]), op0=MUL, op1=SUB)
                dve.scalar_tensor_tensor(out=pooled[:, :, 16:TP], in0=win[:, :, CACHE + 16:CACHE + TP], scalar=inv,
                                         in1=uu[:, g % 2, :, CACHE + 16:CACHE + TP], op0=MUL, op1=SUB)
                dve.wait_ge(fix_ready, g + 1)
                dve.tensor_tensor(pooled[:, :, 0:16], pooled[:, :, 0:16], uu[:, g % 2, :, CACHE:CACHE + 16], SUB)\
                   .then_inc(pooled_ready, 1)

            def pool_lo(g):
                for ct, bk in enumerate((SA, SB)):
                    j = 2 * g + ct
                    dve.wait_ge(mp_hi_s, j + 1)
                    dve.scalar_tensor_tensor(out=bp_lo[:, j, :], in0=bk[:, 0:N], scalar=pcol("pool_scale", j),
                                             in1=bp_hi[:, j, :].bitcast(F32), op0=MUL, op1=SUB).then_inc(mp_lo_s, 1)

            for g in range(NG):
                if g >= 1:
                    split_lo(U0 + 2 * g + 1, 1)
                    pool_means(g - 1)
                if g == 0:
                    lo_piece(U0 + 2, 0, 0, HALF[0])
                    rms_row(1)
                    u_part(0)
                    lo_piece(U0 + 2, 0, 1, HALF[1])
                else:
                    u_part(2 * g)
                    split_lo(U0 + 2 * g + 2, 0)
                if g >= 1:
                    pool_lo(g - 1)
                u_part(2 * g + 1)

            def products(h):
                dve.wait_ge(f_ready, h + 1)
                after(dve, sdec_ready, h)
                after(dve, kx_ready, (LP + 1) * h)
                for l in range(LP):
                    if l:
                        dve.wait_ge(prod_ready, LP * h + l)
                    m = (N if l < LS else TP) // 2 ** (l + 1)
                    dve.tensor_tensor(tl[l + 1][:, 0:m // 2, 1:3], prod_in(l, 1), prod_in(l, 2), MUL)\
                       .then_inc(prod_ready, 1)

            def queries(h):
                dve.wait_ge(q_ready, h + 1)
                after(dve, o_mm, h)
                dve.tensor_tensor(qr[0][:, :].rearrange("p (m a) -> p m a", a=2),
                                  qq[:, :].rearrange("p (m a) -> p m a", a=2), tl[0][:, :, 1:3], MUL)\
                   .then_inc(qr_ready, 1)
                for l in range(LP):
                    n = N if l < LS else TP
                    dve.wait_ge(qr_ready, (LP + 1) * h + l + 1)
                    dve.tensor_tensor(blocks_of(qr[l + 1], l, n), blocks_of(qr[l], l, n), times(l, n, 0), MUL)\
                       .then_inc(qr_ready, 1)

            def mask(col, n, l, rows=P):
                m = cst[0:rows, col:col + n].bitcast(U32)
                return m.rearrange("p (m j) -> p m j", j=2 ** l)

            def rec_scores(r):
                puts = [PUTS * r]

                def put(out, where, src):
                    after(dve, sc_put, puts[0])
                    dve.sem_inc(put_go, 1)
                    dve.copy_predicated(out, where, src).then_inc(sc_put, 1)
                    puts[0] = puts[0] + 1

                def put_level(bk, at_, l):
                    put(right_half(sc[:, :, :].rearrange("p c t -> p (c t)"), l), mask(C_MP + l * P, P, l),
                        bk[:, at_:at_ + P].rearrange("p (m j) -> p m j", j=2 ** l))

                after(dve, o_mm, r)
                dve.wait_ge(sc_mm, 3 * r + 1)
                for l in range(4, LP):
                    put_level(SC, (l - 4) * P, l)
                dve.wait_ge(sc_mm, 3 * r + 2)
                put(sc[:, :, :], ident.bitcast(U32).unsqueeze(1).to_broadcast([P, NC, CH]),
                    SA[:, 0:TP].rearrange("p (c t) -> p c t", c=NC))
                put(scs[:, :], ident[0:NS, 0:NS].bitcast(U32), SA[0:NS, TP:N])
                for l in range(LS):
                    put(right_half(scs[:, :], l), mask(C_MS + 32 * l, 32, l, NS),
                        SA[0:NS, N + 32 * l:N + 32 * l + 32].rearrange("p (m j) -> p m j", j=2 ** l))
                dve.wait_ge(sc_mm, 3 * r + 3)
                for l in range(4):
                    put_level(SB, l * P, l)

            def rec_sample_lo(r):
                for rows, t3, bk, ready, signal in ((slice(2 * HS, 3 * HS), v3, TV, vt_ready, v3_lo),
                                                    (slice(HS, 2 * HS), k3, TK, kt_ready, k3_lo)):
                    dve.wait_ge(ready, r + 1)
                    split_rest(t3[rows, :, :], bk[rows, TP:TP + 2 * P].rearrange("p (i v) -> p i v", i=2),
                               t3[rows, :, :]).then_inc(signal, 1)

            def rec_state(r):
                dve.wait_ge(st_mm, r + 1)
                after(dve, s2_stored, 16 * r)
                dve.tensor_copy(s1[:, :], SC[:, 0:P]).then_inc(s1_ready, 1)
                dve.wait_ge(s1_ready, r + 1)
                dve.scalar_tensor_tensor(out=s2[:, :], in0=s1[:, :], scalar=tl[LP][:, 0, 2:3],
                                         in1=SC[:, P:2 * P], op0=MUL, op1=ADD).then_inc(s2_ready, 1)

            def rec_sample_state(r):
                dve.wait_ge(sn_mm, r + 1)
                dve.wait_ge(sdec_ready, r + 1)
                for i, bk in enumerate((SA, SB)):
                    part = sn[:, 4 * i:4 * i + 4, :]
                    last = dve.tensor_tensor(part, part, bk[:, :].rearrange("p (b v) -> p b v", v=P), ADD)
                last.then_inc(sn_ready, 1)

            def rec_rms(r):
                dve.wait_ge(ostd, r + 1)
                after(dve, obc_mm, r)
                dve.reciprocal(stat[:, 3:6], stat[:, 0:3]).then_inc(orec, 1)
                dve.wait_ge(orec, r + 1)
                newtons[0] = 4 * (r + 1)
                newton(stat[:, 3:6], stat[:, 6:9], stat[:, 9:12])
                diagonals(3, odiag)

            def rec_norm(r):
                dve.wait_ge(obc_mm, r + 1)
                after(dve, mh_hi_s, r)
                dve.scalar_tensor_tensor(out=on[:, :], in0=osb[:, :], scalar=pcol("hg_norm", r), in1=OT[:, 0:N],
                                         op0=MUL, op1=MUL).then_inc(on_ready, 1)

            def rec_lo(r):
                dve.wait_ge(mh_hi_s, r + 1)
                split_rest(bh_lo[:, r, :], on[:, :], bh_hi[:, r, :]).then_inc(mh_lo_s, 1)

            def gate(n, par_, h):
                gate_read(n, par_)
                gate_apply(h)

            def gate_read(n, par_):
                scaled(n, par_, zf[:, :]).then_inc(unit_read, 1)

            def gate_apply(h):
                after(dve, gm_lo, h)
                dve.tensor_tensor(go[:, :], bh_hi[:, h, :].bitcast(F32), bh_lo[:, h, :].bitcast(F32), ADD)\
                   .then_inc(osum, 1)
                dve.wait_ge(osum, h + 1)
                dve.wait_ge(g_act, h + 1)
                dve.tensor_tensor(go[:, :], go[:, :], zq[:, :], MUL).then_inc(gated, 1)
                dve.wait_ge(gm_hi, h + 1)
                split_rest(bh_lo[:, h, :], go[:, :], bh_hi[:, h, :]).then_inc(gm_lo, 1)

            def window(n, par_, h, r):
                split_lo(n + 1, 1 - par_)
                if r is not None:
                    rec_scores(r)
                    rec_sample_lo(r)
                scaled(n, par_, zf[:, :]).then_inc(unit_read, 1)
                if r is not None:
                    rec_state(r)
                if h is None:
                    gate_apply(0)
                split_lo(n + 2, par_)
                if r is not None:
                    rec_sample_state(r)
                else:
                    pool_means(NG - 1)
                    dve.wait_ge(t_ones, 1)
                if h is not None:
                    products(h)
                    scaled(n + 1, 1 - par_, zq[:, :]).then_inc(unit_read, 1)
                else:
                    gate(n + 1, 1 - par_, 1)
                split_lo(n + 3, 1 - par_)
                if r is not None:
                    rec_rms(r)
                if h is not None:
                    queries(h)
                if h is not None:
                    if r is None:
                        pool_lo(NG - 1)
                        dve.wait_ge(sc_zero, 1)
                    done(n + 2)
                    out, src = thrice(v_rep, zb[par_])
                    dve.tensor_tensor(out, src, thrice(v_rep, rbc)[1], MUL).then_inc(v_thrice, 1)
                    scaled(n + 2, par_, vv[:, :]).then_inc(unit_read, 1)
                else:
                    gate(n + 2, par_, 2)
                if h is not None and r is not None:
                    rec_norm(r)
                    rec_lo(r)

            window(H0, 0, 0, None)
            window(H0 + 3, 1, 1, 0)
            with dve.Fori(0, (HEADS - 2) // 2) as i:
                window(H0 + 6 + 6 * i, 0, 2 * i + 2, 2 * i + 1)
                window(H0 + 9 + 6 * i, 1, 2 * i + 3, 2 * i + 2)
            window(G0, 0, None, HEADS - 1)
            split_lo(G0 + 4, 0)
            gate_read(G0 + 3, 1)
            rec_norm(HEADS - 1)
            rec_lo(HEADS - 1)
            gate_apply(3)
            with dve.Fori(0, (HEADS - 4) // 2) as i:
                for k in range(2):
                    split_lo(G0 + 5 + 2 * i + k, 1 - k)
                    gate(G0 + 4 + 2 * i + k, k, 4 + 2 * i + k)

            with dve.Fori(0, KD // 2) as i:
                for k in range(2):
                    j = 2 * i + k
                    split_lo(O0 + 1 + j, 1 - k)
                    done(O0 + j)
                    dve.tensor_tensor(x1[:, j, :], x1[:, j, :], zb[k][:, 0:N], ADD).then_inc(unit_read, 1)
                    dve.wait_ge(h2_hi, j + 1)
                    dve.scalar_tensor_tensor(out=a_lo[:, j, :], in0=x1[:, j, :], scalar=pcol("norm2", j),
                                             in1=a_hi[:, j, :].bitcast(F32), op0=MUL, op1=SUB).then_inc(h2_lo, 1)

            def ffn(b, first, final):
                n0 = F0 + PER_BLOCK * b

                def up(n, c, j):
                    scaled(n, 1, zu[:, :]).then_inc(unit_read, 1)
                    dve.wait_ge(unit_read, n + 1)
                    dve.wait_ge(gate_act, c + 1)
                    dve.tensor_tensor(hid[:, :], zu[:, :], sg[:, :], MUL).then_inc(hid_ready, 1)
                    dve.wait_ge(hid_hi, c + 1)
                    split_rest(h_lo[:, j, :], hid[:, :], h_hi[:, j, :]).then_inc(hid_lo, 1)

                def pair(j, halves):
                    n = n0 + 2 * j
                    split_lo(n + 1, 1)
                    scaled(n, 0, zg[:, :]).then_inc(unit_read, 1)
                    split_lo(n + 2, 0, halves)
                    up(n + 1, KB * b + j, j)
                if first:
                    split_lo(n0 + 1, 1)
                    dve.wait_ge(rms_std, 2)
                    dve.reciprocal(stat[:, 3:6], stat[:, 0:3]).then_inc(orec, 1)
                    dve.wait_ge(orec, HEADS + 1)
                    newtons[0] = 4 * (HEADS + 1)
                    newton(stat[:, 3:6], stat[:, 6:9], stat[:, 9:12])
                    diagonals(3, rms_diag)
                    rms_row(2)
                    scaled(n0, 0, zg[:, :]).then_inc(unit_read, 1)
                    split_lo(n0 + 2, 0)
                    up(n0 + 1, 0, 0)
                with dve.Fori(1 if first else 0, KB - 1) as j:
                    pair(j, HALF)
                pair(KB - 1, HALF_D)
                nd = n0 + 2 * KB

                def down(j, par_):
                    done(nd + j)
                    if final:
                        after(dve, x2_acc, j - 1)
                        after(dve, x2_scaled, j - 1)
                        dve.tensor_tensor(x2[:, par_, :], x1[:, j, :], zb[par_][:, 0:N], ADD).then_inc(unit_read, 1)
                    else:
                        dve.tensor_tensor(x1[:, j, :], x1[:, j, :], zb[par_][:, 0:N], ADD).then_inc(unit_read, 1)

                def down_pair(j):
                    split_lo(nd + 2 * j + 1, 1, HALF_D)
                    down(2 * j, 0)
                    split_lo(nd + 2 * j + 2, 0, HALF_D)
                    down(2 * j + 1, 1)
                if final:
                    down_pair(0)
                with dve.Fori(1 if final else 0, KD // 2 - 1) as j:
                    down_pair(j)
                split_lo(nd + KD - 1, 1, HALF_D)
                down(KD - 2, 0)
                if not final:
                    split_lo(nd + KD, 0)
                down(KD - 1, 1)

            ffn(0, True, False)
            with dve.Fori(1, BLOCKS - 1) as b:
                ffn(b, False, False)
            ffn(BLOCKS - 1, False, True)
            dve.wait_ge(unit_read, F0 + PER_BLOCK * BLOCKS)
            dve.wait_ge(x2_acc, KD - 1)
            dve.tensor_tensor(sq[:, :], x2[:, 1, :], x2[:, 1, :], MUL).then_inc(last_sq, 1)
            dve.wait_ge(rms_std, 3)
            dve.reciprocal(stat[:, 3:6], stat[:, 0:3]).then_inc(y_rec, 1)
            dve.wait_ge(y_rec, 1)
            newtons[0] = 4 * (HEADS + 2)
            newton(stat[:, 3:6], stat[:, 6:9], stat[:, 9:12])
            dve.tensor_copy(stat[:, 9:12], stat[:, 3:6]).then_inc(y_rec, 1)
            dve.wait_ge(y_copied, KD)
            for t, cols in Y_DVE:
                rows = P if t < 2 else NS
                dve.tensor_scalar(yt[0:rows, t, cols], yt[0:rows, t, cols], stat[0:rows, 3 + t:4 + t], None, MUL)\
                   .then_inc(y_scaled_v, 1)

        @block.gpsimd
        def _(pool):
            pool.wait_ge(ss_ready, 6)
            for q in range(2):
                last = pool.memset(uu[:, q, :, 0:CACHE], 0.0)
            last.then_inc(pad_zero, 1)
            pool.wait_ge(xt_t, KD)
            for l in range(LP + 1):
                last = pool.memset(tl[l][:, :, :], 1.0)
            last.then_inc(t_ones, 1)

            steps = 0
            for g, w in enumerate(WINDOWS):
                pool.wait_ge(unit_read, U0 + 2 * g + 2)
                pool.wait_ge(cache_in, g + 1)
                after(pool, pooled_ready, g)
                src, dst, spare, first = uu[:, g % 2], wa, wb, 1
                span = 1
                while span < w:
                    ins = pool.tensor_tensor(dst[:, :, first:UW], src[:, :, first:UW], src[:, :, first - span:UW - span],
                                             ADD)
                    span *= 2
                    if span < w:
                        ins.then_inc(win_step, 1)
                        steps += 1
                        pool.wait_ge(win_step, steps)
                    else:
                        ins.then_inc(win_ready, 1)
                    src, dst, spare, first = dst, spare, dst, first + span

            def rec_sample(r):
                pool.wait_ge(s0_loaded, 16 * (r + 1))
                pool.wait_ge(prod_ready, LP * (r + 1))
                after(pool, sn_stored, 16 * r)
                decay = tl[LS][:, TP // TS // 2:N // TS // 2, 1:3].unsqueeze(3).to_broadcast([P, NB // 2, 2, P])
                pool.tensor_tensor(sn[:, :, :].rearrange("p (m a) v -> p m a v", a=2),
                                   s0[:, :, :].rearrange("p (m a) v -> p m a v", a=2), decay, MUL).then_inc(sdec_ready, 1)
                pool.wait_ge(v3_lo, r + 1)
                after(pool, sn_mm, r)
                shape = [3 * HS, HB, P]
                for i in range(2):
                    last = pool.tensor_tensor(vm[:, i, :, :], v3[:, i:i + 1, :].bitcast(F32).to_broadcast(shape),
                                              cst[0:3 * HS, C_BM:C_BM + HB].unsqueeze(2).to_broadcast(shape), MUL)
                last.then_inc(vm_ready, 1)

            def keys(h):
                pool.wait_ge(f_ready, h + 1)
                after(pool, sc_mm, 3 * h)
                after(pool, k_tr, h)
                pool.tensor_tensor(kx[0][:, :].rearrange("p (m a) -> p m a", a=2),
                                   ones[:, 0:1].unsqueeze(2).to_broadcast([P, N // 2, 2]), tl[0][:, :, 1:3], SUB)\
                    .then_inc(kx_ready, 1)
                for l in range(LP):
                    n = N if l < LS else TP
                    pool.wait_ge(kx_ready, (LP + 1) * h + l + 1)
                    if l:
                        pool.wait_ge(prod_ready, LP * h + l)
                    pool.tensor_tensor(blocks_of(kx[l + 1], l, n), blocks_of(kx[l], l, n), times(l, n, 2), MUL)\
                        .then_inc(kx_ready, 1)

            def query(h):
                pool.wait_ge(zq_sig, h + 1)
                pool.tensor_tensor(qq[:, :], zq[:, :], sgm[:, :], MUL).then_inc(q_ready, 1)

            def key_copies(h):
                pool.wait_ge(kx_ready, (LP + 1) * (h + 1))
                after(pool, obc_mm, h)
                out, src = thrice(k_rep, kx[LS])
                one = ones[:, 0:2].unsqueeze(2).unsqueeze(3).to_broadcast([P, 2, 3, HS])
                pool.tensor_tensor(out, src, one, MUL).then_inc(k_thrice, 1)

            def window(h, r):
                rec_sample(r)
                keys(h)
                query(h)
                key_copies(h)

            pool.wait_ge(fill_done, 3)
            pool.wait_ge(masks_loaded, 16)
            keys(0)
            query(0)
            key_copies(0)
            pool.wait_ge(pooled_ready, NG)
            pool.wait_ge(st_tr, NG)
            pool.wait_ge(pool_mm, 2 * NG)
            pool.memset(sc[:, :, :], 0.0)
            pool.memset(scs[:, :], 0.0).then_inc(sc_zero, 1)
            window(1, 0)
            with pool.Fori(0, (HEADS - 2) // 2) as i:
                window(2 * i + 2, 2 * i + 1)
                window(2 * i + 3, 2 * i + 2)
            rec_sample(HEADS - 1)

            def gate(h):
                pool.wait_ge(g_sig, h + 1)
                pool.tensor_tensor(zq[:, :], zf[:, :], sgm[:, :], MUL).then_inc(g_act, 1)

            for h in range(2):
                gate(h)
            with pool.Fori(0, (HEADS - 2) // 2) as i:
                for k in range(2):
                    gate(2 + 2 * i + k)

            pool.wait_ge(gm_lo, HEADS)
            pool.wait_ge(mh_lo_s, HEADS)
            pool.memset(acc[:, :], 0.0).then_inc(acc_zero, 1)
            pool.wait_ge(acc_zero, 1)
            with pool.Fori(0, KD) as j:
                pool.wait_ge(unit_read, O0 + j + 1)
                pool.tensor_tensor(sq[:, :], x1[:, j, :], x1[:, j, :], MUL).then_inc(x1_sq, 1)
                pool.wait_ge(x1_sq, j + 1)
                pool.tensor_tensor(acc[:, :], acc[:, :], sq[:, :], ADD).then_inc(x1_acc, 1)
                pool.wait_ge(x1_acc, j + 1)
            pool.wait_ge(stat_mm, 1)
            pool.memset(acc[:, :], 0.0).then_inc(acc_zero, 1)
            pool.wait_ge(acc_zero, 2)
            nd = F0 + PER_BLOCK * (BLOCKS - 1) + 2 * KB
            def x2_squares(j, k):
                pool.wait_ge(unit_read, nd + j + 1)
                pool.tensor_tensor(sq[:, :], x2[:, k, :], x2[:, k, :], MUL).then_inc(x2_sq, 1)
                pool.wait_ge(x2_sq, j + 1)
                pool.tensor_tensor(acc[:, :], acc[:, :], sq[:, :], ADD).then_inc(x2_acc, 1)
                pool.wait_ge(x2_acc, j + 1)

            with pool.Fori(0, KD // 2 - 1) as i:
                for k in range(2):
                    x2_squares(2 * i + k, k)
            x2_squares(KD - 2, 0)


INS = ["x_prompt", "x_sample", "cache_pool", "state_hgrn", "lb_param", "norm1", "w_in", "w_pool", "pool_scale",
       "hg_norm", "w_o", "norm2", "w_gate", "w_up", "w_down", "norm_f"]
OUTS = [(1, TP, D), (NB, TS, D), (1, 1, CACHE, PW), (1, 1, HEADS, P, P), (1, NB, CACHE, PW), (1, NB, HEADS, P, P)]


def kernel(**inputs):
    import numpy as np
    import concourse.bacc as bacc
    from concourse.bass_utils import run_bass_kernel_spmd as run

    nc = bacc.Bacc("TRN2", target_bir_lowering=False, num_devices=1)
    arrays = {f"in_{name}": np.ascontiguousarray(inputs[name]) for name in INS}
    arrays["in_consts"] = constant_table(np)
    args = [nc.dram_tensor(n, a.shape, mybir.dt.from_np(a.dtype), kind="ExternalInput").ap() for n, a in arrays.items()]
    args += [nc.dram_tensor(f"out_{i}", s, F32, kind="ExternalOutput").ap() for i, s in enumerate(OUTS)]
    hybrid_kernel(nc, *args)
    r = run(nc, [arrays], core_ids=[0])
    return tuple(r.results[0][f"out_{i}"] for i in range(len(OUTS)))
```
